# Optimizing a Trainium2 kernel written in Bass

```python
import jax, jax.numpy as jnp
from jax import lax
import numpy as np

D_MODEL = 1024
BATCH = 1
SEQ = 1024
DEPTH = 1

HEAD_DIM = 64
N_HEADS_DIL = 8
N_HEADS_NA = 8
D_DIL = N_HEADS_DIL * HEAD_DIM
D_NA = N_HEADS_NA * HEAD_DIM
D_MIX = D_DIL + D_NA
DIL_PATTERNS = ((128, 1), (512, 4), (2048, 16))
DIL_BLOCK = 64
GRID_W = 64
NA_KH = 8
NA_KW = 16
NA_QCB = NA_KW
NA_KCB = 2 * NA_KW
D_FF = 2816
N_MOD = 9
DEEPNORM_ALPHA = (2.0 * DEPTH) ** 0.25
DEEPNORM_BETA = (8.0 * DEPTH) ** -0.25
LN_EPS = 1e-5
NEG_INF = -1e30

kernel_name = "hybrid_dilated_neighbourhood_macaron_encoder"

def _layer_norm(x):
    xf = x.astype(jnp.float32)
    mu = jnp.mean(xf, axis=-1, keepdims=True)
    var = jnp.mean(jnp.square(xf - mu), axis=-1, keepdims=True)
    return (xf - mu) * lax.rsqrt(var + LN_EPS)

def _swiglu(u, w_gate, w_up, w_down):
    return (jax.nn.silu(u @ w_gate) * (u @ w_up)) @ w_down

def _alibi_slopes(n):
    return 2.0 ** (-8.0 * jnp.arange(1, n + 1, dtype=jnp.float32) / n)

def _dilated_branch(q, k, v, slopes, window, dilation):
    B, S, H, Dh = q.shape
    QB = DIL_BLOCK
    radius = window // (2 * dilation)
    L = -(-S // dilation)
    Lp = -(-L // QB) * QB
    nb = Lp // QB
    pad = Lp * dilation - S

    def to_sub(a):
        a = jnp.pad(a, ((0, 0), (0, pad), (0, 0), (0, 0)))
        return a.reshape(B, Lp, dilation, H, Dh).transpose(0, 2, 1, 3, 4)

    def band(a):
        a = jnp.pad(a, ((0, 0), (0, 0), (QB, QB), (0, 0), (0, 0)))
        a = a.reshape(B, dilation, nb + 2, QB, H, Dh)
        return jnp.concatenate([a[:, :, :-2], a[:, :, 1:-1], a[:, :, 2:]], axis=3)

    qb = to_sub(q).reshape(B, dilation, nb, QB, H, Dh)
    kw = band(to_sub(k))
    vw = band(to_sub(v))

    s = jnp.einsum('brinhe,brimhe->brihnm', qb, kw).astype(jnp.float32) * (Dh ** -0.5)
    n_idx = jnp.arange(QB)
    m_idx = jnp.arange(3 * QB)
    rel = m_idx[None, :] - QB - n_idx[:, None]
    jk = (jnp.arange(nb)[:, None] - 1) * QB + m_idx[None, :]
    tk = jk[None] * dilation + jnp.arange(dilation)[:, None, None]
    key_ok = (jk[None] >= 0) & (tk < S)
    valid = (jnp.abs(rel) <= radius)[None, None] & key_ok[:, :, None, :]
    bias = -slopes[:, None, None] * (dilation * jnp.abs(rel)).astype(jnp.float32)
    s = jnp.where(valid[None, :, :, None], s + bias, NEG_INF)
    mx = jnp.max(s, axis=-1, keepdims=True)
    p = jnp.exp(s - mx)
    l = jnp.sum(p, axis=-1, keepdims=True)
    o = jnp.einsum('brihnm,brimhe->brinhe', p.astype(v.dtype), vw).astype(jnp.float32)
    o = o / jnp.swapaxes(l, 3, 4)
    lse = jnp.swapaxes((mx + jnp.log(l))[..., 0], 3, 4)

    def from_sub(a):
        tail = a.shape[4:]
        a = a.reshape((B, dilation, Lp) + tail)
        a = jnp.moveaxis(a, 1, 2).reshape((B, Lp * dilation) + tail)
        return a[:, :S]

    return from_sub(o), from_sub(lse)

def _dilated_attention(q, k, v):
    slopes = _alibi_slopes(q.shape[2])
    outs, lses = [], []
    for window, dilation in DIL_PATTERNS:
        o, lse = _dilated_branch(q, k, v, slopes, window, dilation)
        outs.append(o)
        lses.append(lse)
    w = jax.nn.softmax(jnp.stack(lses, axis=0), axis=0)
    return jnp.einsum('pbsh,pbshe->bshe', w, jnp.stack(outs, axis=0))

def _neighbourhood_attention(q, k, v, rpb):
    B, S, H, Dh = q.shape
    rows = S // GRID_W
    kh = min(NA_KH, rows)
    qg = q.reshape(B, rows, GRID_W, H, Dh)
    kg = k.reshape(B, rows, GRID_W, H, Dh)
    vg = v.reshape(B, rows, GRID_W, H, Dh)
    r = jnp.arange(rows)
    row_start = jnp.clip(r - kh // 2, 0, rows - kh)
    row_idx = row_start[:, None] + jnp.arange(kh)[None, :]
    kr = kg[:, row_idx]
    vr = vg[:, row_idx]
    dr = row_idx - r[:, None]
    bias_rows = rpb[:, dr + NA_KH - 1]
    outs = []
    for cb in range(GRID_W // NA_QCB):
        c0 = cb * NA_QCB
        kc0 = min(max(c0 - NA_KW // 2, 0), GRID_W - NA_KCB)
        qcols = c0 + jnp.arange(NA_QCB)
        kcols = kc0 + jnp.arange(NA_KCB)
        col_start = jnp.clip(qcols - NA_KW // 2, 0, GRID_W - NA_KW)
        colmask = (kcols[None, :] >= col_start[:, None]) & (kcols[None, :] < col_start[:, None] + NA_KW)
        dc_idx = jnp.clip(kcols[None, :] - qcols[:, None] + NA_KW - 1, 0, 2 * NA_KW - 2)
        bias = bias_rows[..., dc_idx].transpose(1, 0, 3, 2, 4)
        qblk = qg[:, :, c0:c0 + NA_QCB]
        kblk = kr[:, :, :, kc0:kc0 + NA_KCB]
        vblk = vr[:, :, :, kc0:kc0 + NA_KCB]
        s = jnp.einsum('brqhe,brkche->brhqkc', qblk, kblk).astype(jnp.float32) * (Dh ** -0.5)
        s = jnp.where(colmask[:, None, :], s + bias, NEG_INF)
        p = jax.nn.softmax(s, axis=(-2, -1))
        outs.append(jnp.einsum('brhqkc,brkche->brqhe', p.astype(v.dtype), vblk))
    return jnp.concatenate(outs, axis=2).reshape(B, S, H, Dh)

def _mixer(u, w_in, rpb, w_out):
    B, S, _ = u.shape
    proj = u @ w_in
    cuts = [D_DIL, 2 * D_DIL, 3 * D_DIL, 3 * D_DIL + D_NA, 3 * D_DIL + 2 * D_NA]
    qa, ka, va, qb, kb, vb = jnp.split(proj, cuts, axis=-1)
    heads_a = lambda t: t.reshape(B, S, N_HEADS_DIL, HEAD_DIM)
    heads_b = lambda t: t.reshape(B, S, N_HEADS_NA, HEAD_DIM)
    ya = _dilated_attention(heads_a(qa), heads_a(ka), heads_a(va)).astype(u.dtype).reshape(B, S, D_DIL)
    yb = _neighbourhood_attention(heads_b(qb), heads_b(kb), heads_b(vb), rpb).astype(u.dtype).reshape(B, S, D_NA)
    return jnp.concatenate([ya, yb], axis=-1) @ w_out

def setup_inputs(seed: int = 0) -> dict:
    key = jax.random.key(seed)
    ks = jax.random.split(key, 20)
    f32 = jnp.float32
    L, D = DEPTH, D_MODEL

    def nrm(k, shape, scale):
        return jax.random.normal(k, shape, f32) * scale

    x = nrm(ks[0], (BATCH, SEQ, D), 1.0)
    c = nrm(ks[1], (BATCH, D), 1.0)
    w_ada = nrm(ks[2], (L, D, N_MOD * D), D ** -0.5)
    b_ada = nrm(ks[3], (L, N_MOD * D), 0.02)
    ffn1_w_gate = nrm(ks[4], (L, D, D_FF), D ** -0.5 * DEEPNORM_BETA)
    ffn1_w_up = nrm(ks[5], (L, D, D_FF), D ** -0.5 * DEEPNORM_BETA)
    ffn1_w_down = nrm(ks[6], (L, D_FF, D), D_FF ** -0.5 * DEEPNORM_BETA)
    qk_a = nrm(ks[7], (L, D, 2 * D_DIL), D ** -0.5)
    v_a = nrm(ks[8], (L, D, D_DIL), D ** -0.5 * DEEPNORM_BETA)
    qk_b = nrm(ks[9], (L, D, 2 * D_NA), D ** -0.5)
    v_b = nrm(ks[10], (L, D, D_NA), D ** -0.5 * DEEPNORM_BETA)
    w_in = jnp.concatenate([qk_a, v_a, qk_b, v_b], axis=-1)
    rpb = nrm(ks[11], (L, N_HEADS_NA, 2 * NA_KH - 1, 2 * NA_KW - 1), 0.1)
    w_out = nrm(ks[12], (L, D_MIX, D), D_MIX ** -0.5 * DEEPNORM_BETA)
    ffn2_w_gate = nrm(ks[13], (L, D, D_FF), D ** -0.5 * DEEPNORM_BETA)
    ffn2_w_up = nrm(ks[14], (L, D, D_FF), D ** -0.5 * DEEPNORM_BETA)
    ffn2_w_down = nrm(ks[15], (L, D_FF, D), D_FF ** -0.5 * DEEPNORM_BETA)
    ln_g = 1.0 + nrm(ks[16], (L, 3, D), 0.02)
    ln_b = nrm(ks[17], (L, 3, D), 0.02)
    return {"x": x, "c": c, "w_ada": w_ada, "b_ada": b_ada,
            "ffn1_w_gate": ffn1_w_gate, "ffn1_w_up": ffn1_w_up, "ffn1_w_down": ffn1_w_down,
            "w_in": w_in, "rpb": rpb, "w_out": w_out,
            "ffn2_w_gate": ffn2_w_gate, "ffn2_w_up": ffn2_w_up, "ffn2_w_down": ffn2_w_down,
            "ln_g": ln_g, "ln_b": ln_b}

def reference(x, c, w_ada, b_ada, ffn1_w_gate, ffn1_w_up, ffn1_w_down, w_in, rpb, w_out,
              ffn2_w_gate, ffn2_w_up, ffn2_w_down, ln_g, ln_b):
    h = x
    for layer in range(DEPTH):
        mods = (jax.nn.silu(c) @ w_ada[layer] + b_ada[layer]).reshape(c.shape[0], N_MOD, D_MODEL)

        def sublayer(h, j, fn, resid_w):
            shift = mods[:, 3 * j][:, None]
            scale = mods[:, 3 * j + 1][:, None]
            gate = mods[:, 3 * j + 2][:, None]
            u = (_layer_norm(h) * (1.0 + scale) + shift).astype(h.dtype)
            z = DEEPNORM_ALPHA * h.astype(jnp.float32) + resid_w * gate * fn(u)
            return (_layer_norm(z) * ln_g[layer, j] + ln_b[layer, j]).astype(h.dtype)

        h = sublayer(h, 0, lambda u: _swiglu(u, ffn1_w_gate[layer], ffn1_w_up[layer], ffn1_w_down[layer]), 0.5)
        h = sublayer(h, 1, lambda u: _mixer(u, w_in[layer], rpb[layer], w_out[layer]), 1.0)
        h = sublayer(h, 2, lambda u: _swiglu(u, ffn2_w_gate[layer], ffn2_w_up[layer], ffn2_w_down[layer]), 0.5)
    return h


_drawn_inputs = setup_inputs


def setup_inputs(seed=0):
    import zlib

    import numpy as np

    out = dict(_drawn_inputs(seed))
    spreads = {}
    factors = {'b_ada': 8.0, 'rpb': 8.0}
    for name, (base, spread) in spreads.items():
        noise = np.random.default_rng([zlib.crc32(name.encode()), seed]).standard_normal(out[name].shape)
        drawn = base * np.exp(spread * noise) if base else spread * noise
        out[name] = __import__('jax').numpy.asarray(drawn.astype(out[name].dtype))
    for name, factor in factors.items():
        out[name] = (out[name] * factor).astype(out[name].dtype)
    return out
```

```python
from contextlib import ExitStack

import concourse.bass as bass
import concourse.mybir as mybir
import numpy as np

F32 = mybir.dt.float32
F32R = mybir.dt.float32r
ALU = mybir.AluOpType
ACT = mybir.ActivationFunctionType
AX = mybir.AxisListType

P = 128
S = 1024
D = 1024
F = 2816
N_MOD = 9
KT = D // P
TT = S // P
NB = 512
HALVES = S // NB
FC = F // P
PAIRS = FC // 2
ALPHA = 2.0 ** 0.25
EPS = 1e-5
HD = 64
HEADS = 8
HP = HEADS // 2
BIG = 1e30

CL = 4
CQ = P // CL
CK = S // CL
BAND = 256
BAND_W = 384
CLS_W = CK + CK - CQ
A_W = BAND_W + CLS_W
A_PAD = 2 * A_W + 256
NAT = (0, 1, TT - 2, TT - 1)
OFFS = tuple(range(HD, S - P - HD + 1, P))
A_VT = len(NAT) + len(OFFS) + 2 * CL

ROWS, COLS = 16, 64
QR, QC = 8, 16
KH, KW = 8, 16
KR, KC = 12, 32
B_K = KR * KC
CBS = COLS // QC
RBS = ROWS // QR
RC = 4
TAB_R, TAB_W = 23, 64
RUN_R = 16
RUN = (RUN_R - 1) * TAB_W + 48
KC0 = tuple(min(max(QC * c - KW // 2, 0), COLS - KC) for c in range(CBS))
KIND = (0, 1, 1, 2)


def slopes():
    return 2.0 ** (-8.0 * np.arange(1, HEADS + 1) / HEADS)


def dilated_bias():
    q = np.arange(P)
    tok = 4 * (q % CQ) + q // CQ
    rel_band = np.arange(BAND_W)[None, :] - P - tok[:, None]
    rel_cls = np.arange(CLS_W)[None, :] - (CK - CQ) - (q % CQ)[:, None]
    count = (np.abs(rel_cls) <= 64).astype(np.float64) + (rel_cls % 4 == 0)
    out = np.zeros((P, HP, A_PAD), np.float32)
    for h, s in enumerate(slopes()):
        band = np.where(np.abs(rel_band) <= 64, s * np.abs(rel_band), BIG)
        cls = np.where(count > 0, s * 4 * np.abs(rel_cls) - np.log(np.maximum(count, 1)), BIG)
        at = (h % 2) * A_W
        out[:, h // 2, at:at + A_W] = np.concatenate([band, cls], axis=1)
    return out


def window_masks():
    out = np.zeros((P, RBS * 3, KR, KC), np.float32)
    for rb in range(RBS):
        for cb in range(CBS):
            for q in range(P):
                r, c = QR * rb + q // QC, QC * cb + q % QC
                r0 = min(max(r - KH // 2, 0), ROWS - KH)
                c0 = min(max(c - KW // 2, 0), COLS - KW)
                rows = 4 * rb + np.arange(KR)
                cols = KC0[cb] + np.arange(KC)
                ok = ((rows >= r0) & (rows < r0 + KH))[:, None] & ((cols >= c0) & (cols < c0 + KW))
                out[q, rb * 3 + KIND[cb]] = np.where(ok, 0.0, BIG)
    return out.reshape(P, RBS * 3, B_K)


class Parts:

    def __init__(self, nc, stack):
        self.nc, self.stack = nc, stack

    def sb(self, name, shape, dt=F32):
        return self.stack.enter_context(self.nc.sbuf_tensor(name, shape, dt))

    def ps(self, name, shape, dt=F32):
        return self.stack.enter_context(self.nc.psum_tensor(name, shape, dt))

    def sem(self, name):
        return self.nc.alloc_semaphore(name=name)


def modulation_phase(nc, top, c, w_ada, b_ada, ident_in, mods_row, mods_out, mod_col, ident):
    n = 6
    cw = N_MOD * D // n
    tw = cw // 4
    rows = N_MOD * KT
    in_ld, w_ld = top.sem("m_in_ld"), [top.sem(f"m_w_ld{b}") for b in range(2)]
    c_ready, mm_done, row_done = top.sem("m_c_ready"), top.sem("m_mm"), top.sem("m_row")
    row_st, row_ld, sum_done = top.sem("m_row_st"), top.sem("m_row_ld"), top.sem("m_sum")
    tr_done, col_done, out_st = top.sem("m_tr"), top.sem("m_col"), top.sem("m_out_st")
    with ExitStack() as st:
        a = Parts(nc, st)
        w = a.sb("m_w", [P, 2, KT, cw])
        ccol = a.sb("m_c", [P, KT])
        cs = a.sb("m_cs", [P, KT])
        row = a.sb("m_rowbuf", [1, N_MOD * D])
        grid = a.sb("m_grid", [rows, P])
        bgrid = a.sb("m_bgrid", [rows, P])
        sums = a.sb("m_sums", [rows, P])
        acc = a.ps("m_acc", [P, 2, NB])
        turned = a.ps("m_turned", [P, NB])
        block = st.enter_context(nc.Block())

        @block.sync
        def _(sp):
            sp.dma_start(ident[:, :], ident_in).then_inc(in_ld, 16)
            with nc.allow_non_contiguous_dma(reason="one short vector"):
                sp.dma_start(ccol[:, :], c.rearrange("o (k p) -> p (o k)", p=P)).then_inc(in_ld, 16)
            sp.dma_start(bgrid[:, :], b_ada.rearrange("l (r p) -> (l r) p", p=P)).then_inc(in_ld, 16)
            for i in range(n):
                if i >= 2:
                    sp.wait_ge(mm_done, i - 1)
                sp.dma_start(w[:, i % 2], w_ada.rearrange("l (k p) n -> p (l k) n", p=P)
                             [:, :, cw * i:cw * i + cw]).then_inc(w_ld[i % 2], 16)
            sp.wait_ge(row_done, 4 * n)
            sp.dma_start(mods_row, row[:, :]).then_inc(row_st, 16)
            sp.wait_ge(row_st, 16)
            sp.dma_start(grid[:, :], mods_row.rearrange("o (r p) -> (o r) p", p=P)).then_inc(row_ld, 16)
            sp.wait_ge(sum_done, 1)
            sp.dma_start(mods_out.rearrange("o (r p) -> (o r) p", p=P), sums[:, :]).then_inc(out_st, 16)
            sp.wait_ge(out_st, 16)

        @block.scalar
        def _(act):
            act.wait_ge(in_ld, 48)
            nc.scalar.activation(cs[:, :], ccol[:, :], ACT.Silu).then_inc(c_ready, 1)

        @block.tensor
        def _(pe):
            pe.wait_ge(c_ready, 1)
            for i in range(n):
                pe.wait_ge(w_ld[i % 2], 16 * (i // 2 + 1))
                if i >= 2:
                    pe.wait_ge(row_done, 4 * (i - 1))
                for k in range(KT):
                    for j in range(4):
                        last = nc.tensor.matmul(acc[32 * j:32 * j + 1, i % 2, 0:tw], cs[:, k:k + 1],
                                                w[:, i % 2, k, tw * j:tw * j + tw],
                                                start=(k == 0), stop=(k == KT - 1))
                last.then_inc(mm_done, 1)
            pe.wait_ge(sum_done, 1)
            nc.tensor.transpose(turned[:, 0:rows], sums[:, :], ident[0:rows, 0:rows]).then_inc(tr_done, 1)

        @block.vector
        def _(dve):
            for i in range(n):
                dve.wait_ge(mm_done, i + 1)
                for j in range(4):
                    at = cw * i + tw * j
                    nc.vector.tensor_copy(row[0:1, at:at + tw],
                                          acc[32 * j:32 * j + 1, i % 2, 0:tw]).then_inc(row_done, 1)
            dve.wait_ge(row_ld, 16)
            dve.wait_ge(in_ld, 48)
            nc.vector.tensor_tensor(sums[:, :], grid[:, :], bgrid[:, :], ALU.add).then_inc(sum_done, 1)
            dve.wait_ge(tr_done, 1)
            src = turned[:, 0:rows].rearrange("p (j w k) -> p j w k", j=3, w=3)
            dst = mod_col[:, :].rearrange("p (j w k) -> p j w k", j=3, w=2)
            for j in range(3):
                nc.vector.tensor_copy(dst[:, j, 0], src[:, j, 0]).then_inc(col_done, 1)
                nc.vector.tensor_scalar(dst[:, j, 1], src[:, j, 1], 1.0, None, ALU.add).then_inc(col_done, 1)


def boundary_phase(nc, top, tag, h_in, h_out, acc, gate, lng, lnb, resid, enter, mod_col, ident,
                   ut_hi, ut_lo):
    leave = gate is not None
    h_ld = [top.sem(f"{tag}_h_ld{b}") for b in range(2)]
    bc_ld, h_st = top.sem(tag + "_bc_ld"), [top.sem(f"{tag}_h_st{b}") for b in range(2)]
    eps_set, dv, sq = top.sem(tag + "_eps_set"), top.sem(tag + "_dve"), top.sem(tag + "_std")
    var_ready, coef_ready, z_norm = top.sem(tag + "_var"), top.sem(tag + "_coef"), top.sem(tag + "_znorm")
    gained, shifted = top.sem(tag + "_gained"), top.sem(tag + "_shifted")
    n_done, tr_done, mod_done = top.sem(tag + "_n"), top.sem(tag + "_tr"), top.sem(tag + "_mod")
    hi_done, lo_done = top.sem(tag + "_hi"), top.sem(tag + "_lo")
    G = TT // HALVES
    with ExitStack() as st:
        a = Parts(nc, st)
        h = a.sb(tag + "_h", [P, 2, D])
        z = a.sb(tag + "_z", [P, 2, D])
        zn = a.sb(tag + "_zn", [P, 2, D])
        zg = a.sb(tag + "_zg", [P, 2, D])
        hn = a.sb(tag + "_hn", [P, 2, D])
        nrm = a.sb(tag + "_nrm", [P, G, D])
        mod = a.sb(tag + "_mod", [P, 2, NB])
        rows = a.sb(tag + "_rows", [P, 3, D])
        sm = a.sb(tag + "_sm", [P, 2, 2, 24])
        eps = a.sb(tag + "_eps", [P, 1])
        turned = a.ps(tag + "_turned", [P, 2, NB])
        block = st.enter_context(nc.Block())

        if leave:
            new = hn
        else:
            new = h

        @block.sync
        def _(sp):
            if leave:
                for i, r in enumerate((gate, lng, lnb)):
                    sp.dma_start(rows[:, i, :], r.broadcast_to([P, D])).then_inc(bc_ld, 16)
            for t in range(TT):
                if t >= 2:
                    if leave:
                        sp.wait_ge(z_norm, t - 1)
                    else:
                        sp.wait_ge(n_done, t - 1)
                sp.dma_start(h[:, t % 2, :], h_in[P * t:P * t + P, :]).then_inc(h_ld[t % 2], 16)
            if leave:
                for b in range(2):
                    sp.wait_ge(h_st[b], 16 * TT // 2)

        @block.gpsimd
        def _(pool):
            if leave:
                pool.wait_ge(bc_ld, 48)
                for t in range(TT):
                    pool.wait_ge(z_norm, t + 1)
                    if t >= 2:
                        pool.wait_ge(shifted, t - 1)
                    nc.gpsimd.tensor_tensor(zg[:, t % 2, :], zn[:, t % 2, :], rows[:, 1, :],
                                            ALU.mult).then_inc(gained, 1)

        @block.scalar
        def _(act):
            act.wait_ge(eps_set, 1)

            def std(t, ln, n):
                act.wait_ge(var_ready, n)
                nc.scalar.activation(sm[:, t % 2, ln, 14:15], sm[:, t % 2, ln, 13:14], ACT.Sqrt,
                                     bias=eps[:, 0:1]).then_inc(sq, 1)

            per = (1 if leave else 0) + (1 if enter is not None else 0)
            for t in range(TT):
                n = per * t
                if leave:
                    n += 1
                    std(t, 0, n)
                    act.wait_ge(coef_ready, n)
                    if t >= 2:
                        act.wait_ge(gained, t - 1)
                    nc.scalar.activation(zn[:, t % 2, :], z[:, t % 2, :], ACT.Identity,
                                         bias=sm[:, t % 2, 0, 18:19],
                                         scale=sm[:, t % 2, 0, 17:18]).then_inc(z_norm, 1)
                    act.wait_ge(shifted, t + 1)
                    act.dma_start(h_out[P * t:P * t + P, :], hn[:, t % 2, :]).then_inc(h_st[t % 2], 16)
                if enter is not None:
                    n += 1
                    std(t, 1, n)
                    act.wait_ge(coef_ready, n)
                    if t >= G:
                        act.wait_ge(tr_done, KT)
                    nc.scalar.activation(nrm[:, t % G, :], new[:, t % 2, :], ACT.Identity,
                                         bias=sm[:, t % 2, 1, 18:19],
                                         scale=sm[:, t % 2, 1, 17:18]).then_inc(n_done, 1)
                    if t % G == G - 1:
                        half = t // G
                        for k in range(KT):
                            x = KT * half + k
                            act.wait_ge(mod_done, x + 1)
                            nc.scalar.copy(ut_hi[:, k, NB * half:NB * half + NB],
                                           mod[:, k % 2, :]).then_inc(hi_done, 1)

        @block.tensor
        def _(pe):
            if enter is not None:
                for half in range(HALVES):
                    pe.wait_ge(n_done, G * (half + 1))
                    for k in range(KT):
                        x = KT * half + k
                        if x >= 2:
                            pe.wait_ge(mod_done, x - 1)
                        for g in range(G):
                            last = nc.tensor.transpose(turned[:, x % 2, P * g:P * g + P],
                                                       nrm[:, g, P * k:P * k + P], ident[:, :])
                        last.then_inc(tr_done, 1)

        @block.vector
        def _(dve):
            count = [0]

            def step(ins, wait=True):
                count[0] += 1
                ins.then_inc(dv, 1)
                if wait:
                    dve.wait_ge(dv, count[0])

            def ln_stats(x, t, ln):
                s_ = sm[:, t % 2, ln, :]
                step(nc.vector.bn_stats(s_[:, 0:6], x[:, 0:NB]), wait=False)
                step(nc.vector.bn_stats(s_[:, 6:12], x[:, NB:D]))
                seen[0] += 1
                nc.vector.bn_aggr(s_[:, 12:14], s_[:, 0:12]).then_inc(var_ready, 1)
                dve.wait_ge(sq, seen[0])
                step(nc.vector.reciprocal(s_[:, 15:16], s_[:, 14:15]))
                step(nc.vector.tensor_scalar(s_[:, 19:20], s_[:, 13:14], EPS, None, ALU.add))
                step(nc.vector.tensor_scalar(s_[:, 16:17], s_[:, 15:16], s_[:, 15:16],
                                             s_[:, 19:20], ALU.mult, ALU.mult))
                step(nc.vector.tensor_scalar(s_[:, 20:21], s_[:, 16:17], -0.5, 1.5, ALU.mult, ALU.add))
                step(nc.vector.tensor_scalar(s_[:, 17:18], s_[:, 15:16], s_[:, 20:21], None, ALU.mult))
                nc.vector.tensor_scalar(s_[:, 18:19], s_[:, 12:13], s_[:, 17:18], -1.0,
                                        ALU.mult, ALU.mult).then_inc(coef_ready, 1)

            seen = [0]
            nc.vector.memset(eps[:, :], EPS).then_inc(eps_set, 1)
            if leave:
                dve.wait_ge(bc_ld, 48)
            for t in range(TT):
                dve.wait_ge(h_ld[t % 2], 16 * (t // 2 + 1))
                if leave:
                    step(nc.vector.scalar_tensor_tensor(acc[:, t, :], acc[:, t, :], resid, rows[:, 0, :],
                                                        ALU.mult, ALU.mult))
                    if t >= 2:
                        dve.wait_ge(z_norm, t - 1)
                    step(nc.vector.scalar_tensor_tensor(z[:, t % 2, :], h[:, t % 2, :], ALPHA,
                                                        acc[:, t, :], ALU.mult, ALU.add))
                    ln_stats(z[:, t % 2, :], t, 0)
                    dve.wait_ge(gained, t + 1)
                    if t >= 2:
                        dve.wait_ge(h_st[t % 2], 16 * (t // 2))
                        if enter is not None:
                            dve.wait_ge(n_done, t - 1)
                    nc.vector.tensor_tensor(hn[:, t % 2, :], zg[:, t % 2, :], rows[:, 2, :],
                                            ALU.add).then_inc(shifted, 1)
                    dve.wait_ge(shifted, t + 1)
                if enter is not None:
                    if t >= 2:
                        dve.wait_ge(n_done, t - 1)
                    ln_stats(new[:, t % 2, :], t, 1)
                    if t % G == G - 1:
                        half = t // G
                        for k in range(KT):
                            x = KT * half + k
                            dve.wait_ge(tr_done, x + 1)
                            if x >= 2:
                                dve.wait_ge(lo_done, x - 1)
                            m = 16 * enter + k
                            nc.vector.tensor_scalar(mod[:, k % 2, :], turned[:, x % 2, :],
                                                    mod_col[:, m + 8:m + 9], mod_col[:, m:m + 1],
                                                    ALU.mult, ALU.add).then_inc(mod_done, 1)
                            dve.wait_ge(hi_done, x + 1)
                            cols = slice(NB * half, NB * half + NB)
                            nc.vector.tensor_tensor(ut_lo[:, k, cols], mod[:, k % 2, :],
                                                    ut_hi[:, k, cols].bitcast(F32),
                                                    ALU.subtract).then_inc(lo_done, 1)


def ffn_phase(nc, top, tag, w_gate, w_up, w_down, ut_hi, ut_lo, acc):
    ld_gu, ld_d = top.sem(tag + "_ld_gu"), top.sem(tag + "_ld_d")
    w_hi, w_lo = [top.sem(f"{tag}_w_hi{i}") for i in range(2)], [top.sem(f"{tag}_w_lo{i}") for i in range(2)]
    d_hi, d_lo = top.sem(tag + "_d_hi"), top.sem(tag + "_d_lo")
    gu_mm, silu_done, mul_done = top.sem(tag + "_gu_mm"), top.sem(tag + "_silu"), top.sem(tag + "_mul")
    hid_hi_s, hid_lo_s = top.sem(tag + "_hid_hi"), top.sem(tag + "_hid_lo")
    d_mm, d_add = top.sem(tag + "_d_mm"), top.sem(tag + "_d_add")
    NT = TT * HALVES
    with ExitStack() as st:
        a = Parts(nc, st)
        raw = a.sb(tag + "_raw", [P, KT, 2, 2 * P])
        raw_d = a.sb(tag + "_raw_d", [P, 2, D])
        wh = a.sb(tag + "_wh", [P, 2, KT, 2, P], F32R)
        wl = a.sb(tag + "_wl", [P, 2, KT, 2, P], F32R)
        dh = a.sb(tag + "_dh", [P, 2, D], F32R)
        dl = a.sb(tag + "_dl", [P, 2, D], F32R)
        hid_hi = a.sb(tag + "_hidh", [P, 2, S], F32R)
        hid_lo = a.sb(tag + "_hidl", [P, 2, S], F32R)
        sil = a.sb(tag + "_sil", [P, 2, NB])
        prod = a.sb(tag + "_prod", [P, 2, NB])
        gu = a.ps(tag + "_gu", [P, 2, 2, NB])
        dp = a.ps(tag + "_dp", [P, 4, NB])
        block = st.enter_context(nc.Block())
        gate_v = w_gate.rearrange("(k p) n -> p k n", p=P)
        up_v = w_up.rearrange("(k p) n -> p k n", p=P)
        down_v = w_down.rearrange("(f p) n -> p f n", p=P)

        @block.sync
        def _(sp):
            def load(q, first):
                if not first:
                    sp.wait_ge(w_lo[1], q)
                cols = bass.ds(q * 2 * P, 2 * P)
                sp.dma_start(raw[:, :, 0, :], gate_v[:, :, cols]).then_inc(ld_gu, 16)
                sp.dma_start(raw[:, :, 1, :], up_v[:, :, cols]).then_inc(ld_gu, 16)
                if not first:
                    sp.wait_ge(d_lo, q)
                sp.dma_start(raw_d[:, :, :], down_v[:, bass.ds(q * 2, 2), :]).then_inc(ld_d, 16)

            load(0, True)
            with sp.Fori(1, PAIRS) as q:
                load(q, False)

        @block.gpsimd
        def _(pool):
            nc.gpsimd.memset(acc[:, :, :], 0.0).then_inc(d_add, NT)

        @block.scalar
        def _(act):
            def split_gu(q, i, first):
                act.wait_ge(ld_gu, 32 * (q + 1))
                if not first:
                    act.wait_ge(gu_mm, 4 * q + 2 * i - 2)
                nc.scalar.copy(wh[:, i], raw[:, :, :, P * i:P * i + P]).then_inc(w_hi[i], 1)

            def split_d(q, first):
                act.wait_ge(ld_d, 16 * (q + 1))
                if not first:
                    act.wait_ge(d_mm, NT * q)
                nc.scalar.copy(dh[:, :, :], raw_d[:, :, :]).then_inc(d_hi, 1)

            def silu(q, i, first):
                for half in range(2):
                    s_ = 4 * q + 2 * i + half
                    act.wait_ge(gu_mm, s_ + 1)
                    if not first:
                        act.wait_ge(mul_done, s_ - 1)
                    nc.scalar.activation(sil[:, half, :], gu[:, half, 0, :],
                                         ACT.Silu).then_inc(silu_done, 1)

            def split_hid(q, i, first):
                for half in range(2):
                    s_ = 4 * q + 2 * i + half
                    act.wait_ge(mul_done, s_ + 1)
                    if not first:
                        act.wait_ge(d_mm, NT * q)
                    nc.scalar.copy(hid_hi[:, i, NB * half:NB * half + NB],
                                   prod[:, half, :]).then_inc(hid_hi_s, 1)

            def body(q, ahead):
                silu(q, 0, False)
                if ahead:
                    split_gu(q + 1, 0, False)
                split_hid(q, 0, False)
                split_d(q, False)
                silu(q, 1, False)
                split_hid(q, 1, False)
                if ahead:
                    split_gu(q + 1, 1, False)

            for i in range(2):
                split_gu(0, i, True)
            silu(0, 0, True)
            split_gu(1, 0, False)
            split_hid(0, 0, True)
            split_d(0, True)
            silu(0, 1, False)
            split_hid(0, 1, True)
            split_gu(1, 1, False)
            with act.Fori(1, PAIRS - 1) as q:
                body(q, True)
            body(PAIRS - 1, False)

        @block.vector
        def _(dve):
            def split_gu(q, i):
                dve.wait_ge(w_hi[i], q + 1)
                nc.vector.tensor_tensor(wl[:, i], raw[:, :, :, P * i:P * i + P], wh[:, i].bitcast(F32),
                                        ALU.subtract).then_inc(w_lo[i], 1)

            def split_d(q):
                dve.wait_ge(d_hi, q + 1)
                nc.vector.tensor_tensor(dl[:, :, :], raw_d[:, :, :], dh[:, :, :].bitcast(F32),
                                        ALU.subtract).then_inc(d_lo, 1)

            def mul(q, i, first):
                for half in range(2):
                    s_ = 4 * q + 2 * i + half
                    dve.wait_ge(silu_done, s_ + 1)
                    if not first:
                        dve.wait_ge(hid_lo_s, s_ - 1)
                    nc.vector.tensor_tensor(prod[:, half, :], sil[:, half, :], gu[:, half, 1, :],
                                            ALU.mult).then_inc(mul_done, 1)

            def split_hid(q, i):
                for half in range(2):
                    s_ = 4 * q + 2 * i + half
                    cols = slice(NB * half, NB * half + NB)
                    dve.wait_ge(hid_hi_s, s_ + 1)
                    nc.vector.tensor_tensor(hid_lo[:, i, cols], prod[:, half, :],
                                            hid_hi[:, i, cols].bitcast(F32),
                                            ALU.subtract).then_inc(hid_lo_s, 1)

            def add_down(q):
                for j in range(NT):
                    t, half = j // 2, j % 2
                    cols = slice(NB * half, NB * half + NB)
                    dve.wait_ge(d_mm, NT * q + j + 1)
                    dve.wait_ge(d_add, NT * q + j + 1)
                    nc.vector.tensor_tensor(acc[:, t, cols], dp[:, j % 4, :], acc[:, t, cols],
                                            ALU.add).then_inc(d_add, 1)

            def body(q, ahead):
                mul(q, 0, False)
                if ahead:
                    split_gu(q + 1, 0)
                add_down(q - 1)
                split_hid(q, 0)
                split_d(q)
                mul(q, 1, False)
                split_hid(q, 1)
                if ahead:
                    split_gu(q + 1, 1)

            for i in range(2):
                split_gu(0, i)
            mul(0, 0, True)
            split_gu(1, 0)
            split_hid(0, 0)
            split_d(0)
            mul(0, 1, False)
            split_hid(0, 1)
            split_gu(1, 1)
            dve.wait_ge(d_add, NT)
            with dve.Fori(1, PAIRS - 1) as q:
                body(q, True)
            body(PAIRS - 1, False)
            add_down(PAIRS - 1)

        @block.tensor
        def _(pe):
            def gate_up(q, i, first):
                pe.wait_ge(w_lo[i], q + 1)
                for half in range(2):
                    s_ = 4 * q + 2 * i + half
                    cols = slice(NB * half, NB * half + NB)
                    if not first:
                        pe.wait_ge(mul_done, s_ - 1)
                    for g in range(2):
                        for k in range(KT):
                            for n, (l, r) in enumerate(((wh, ut_hi), (wh, ut_lo), (wl, ut_hi))):
                                last = nc.tensor.matmul(gu[:, half, g, :], l[:, i, k, g, :],
                                                        r[:, k, cols], start=(k == 0 and n == 0),
                                                        stop=(k == KT - 1 and n == 2))
                    last.then_inc(gu_mm, 1)

            def down(q, first=False):
                pe.wait_ge(hid_lo_s, 4 * (q + 1))
                pe.wait_ge(d_lo, q + 1)
                for j in range(NT):
                    t, half = j // 2, j % 2
                    pe.wait_ge(d_add, NT * q + j + 13)
                    for i in range(2):
                        for n, (l, r) in enumerate(((hid_hi, dh), (hid_hi, dl), (hid_lo, dh))):
                            last = nc.tensor.matmul(dp[:, j % 4, :], l[:, i, P * t:P * t + P],
                                                    r[:, i, NB * half:NB * half + NB],
                                                    start=(i == 0 and n == 0), stop=(i == 1 and n == 2))
                    last.then_inc(d_mm, 1)

            gate_up(0, 0, True)
            gate_up(0, 1, False)
            with pe.Fori(1, PAIRS) as q:
                gate_up(q, 0, False)
                down(q - 1)
                gate_up(q, 1, False)
            down(PAIRS - 1)


def table_phase(nc, top, rpb, tab):
    zeroed, ld, neg, stored = (top.sem("t_" + n) for n in ("zero", "ld", "neg", "st"))
    nr, nw = rpb.shape[2:]
    with ExitStack() as st:
        a = Parts(nc, st)
        raw = a.sb("t_raw", [HEADS, nr, nw])
        pad = a.sb("t_pad", [HEADS, TAB_R, TAB_W])
        block = st.enter_context(nc.Block())

        @block.sync
        def _(sp):
            sp.dma_start(raw[:, :, :], rpb[0]).then_inc(ld, 16)
            sp.wait_ge(neg, 1)
            flat = pad[:, :, :].rearrange("h r w -> h (r w)")
            for n in range(QC):
                shift = QC - 1 - n
                sp.dma_start(tab[n, :, 0:TAB_R * TAB_W - shift],
                             flat[:, shift:TAB_R * TAB_W]).then_inc(stored, 16)
            sp.wait_ge(stored, 16 * QC)

        @block.vector
        def _(dve):
            nc.vector.memset(pad[:, :, :], 0.0).then_inc(zeroed, 1)
            dve.wait_ge(zeroed, 1)
            dve.wait_ge(ld, 16)
            r0, c0 = (TAB_R - nr) // 2, (TAB_W - 1 - nw) // 2
            nc.vector.tensor_scalar(pad[:, r0:r0 + nr, c0:c0 + nw], raw[:, :, :], -1.0, None,
                                    ALU.mult).then_inc(neg, 1)


def band_start(t):
    return min(max(P * t - HD, 0), S - BAND)


def value_tiles_a():
    return ([(P * n, 1) for n in NAT] + [(o, 1) for o in OFFS]
            + [(CL * P * c + r, CL) for r in range(CL) for c in range(2)])


def products(dil, half):
    out = []
    if not dil:
        for cb in range(CBS // HALVES):
            for rc in range(ROWS // RC):
                users = [(cb * RBS + rb, rc - rb) for rb in range(RBS) if 0 <= rc - rb < KR // RC]
                out.append((rc * CBS + half * CBS // HALVES + cb, users, None))
        return out
    for v, (start, step) in enumerate(value_tiles_a()):
        if step != 1:
            continue
        users = []
        for t in range(TT // HALVES):
            w0 = band_start(half * TT // HALVES + t)
            users += [(t, ch) for ch in range(BAND // P) if w0 + P * ch == start]
        if users:
            out.append((v, users, None))
    for r in range(CL):
        for c in range(CK // P):
            out.append((len(NAT) + len(OFFS) + 2 * r + c, [(t, BAND // P + c) for t in range(TT // HALVES)], r))
    return out


def attention_phase(nc, top, tag, w_in, w_at, y_at, ut_hi, ut_lo, scratch, ident, bias_in, tab, y_t):
    dil = tag == "a"
    NC = 4 if dil else 3
    W = NC * P
    HT = TT // HALVES
    NV = A_VT if dil else (ROWS // RC) * CBS
    VB = 4
    NVG = -(-NV // VB)
    UN = 2 * HT
    NU = HALVES * UN
    NPJ = 3 * HALVES
    LAG = 3

    def sem(name):
        return top.sem(f"{tag}_{name}")

    w_ld, b_ld, w_hi, w_lo = sem("w_ld"), sem("b_ld"), sem("w_hi"), sem("w_lo")
    zeroed, pj_mm, pj_out = sem("zeroed"), sem("pj_mm"), sem("pj_out")
    v_tr, v_out, qk, low, exped = sem("v_tr"), sem("v_out"), sem("qk"), sem("low"), sem("exped")
    rec, divided, p_tr, p_out = sem("rec"), sem("divided"), sem("p_tr"), sem("p_out")
    pv, y_out, y_st, b_ready, r_ld = sem("pv"), sem("y_out"), sem("y_st"), sem("b_ready"), sem("r_ld")
    with ExitStack() as st:
        a = Parts(nc, st)
        raw = a.sb(tag + "_raw", [P, KT, 3, P])
        wh = a.sb(tag + "_wh", [P, KT, 3, P], F32R)
        wl = a.sb(tag + "_wl", [P, KT, 3, P], F32R)
        q = a.sb(tag + "_q", [P, 2, S])
        kv = a.sb(tag + "_kv", [P, 2 if dil else 1, S])
        t_s = a.sb(tag + "_t", [P, 2, W])
        ex = a.sb(tag + "_ex", [P, 2, W])
        pn = a.sb(tag + "_pn", [P, 2, W])
        sm = a.sb(tag + "_sm", [P, 2, 4])
        y = a.sb(tag + "_y", [P, S])
        if dil:
            kc = a.sb("a_kc", [P, CL, CK])
            bias = a.sb("a_bias", [P, A_PAD])
        else:
            runs = a.sb("b_runs", [P, 2, RUN_R * TAB_W])
            mask = a.sb("b_mask", [P, RBS * 3, B_K])
            bias = a.sb("b_bias", [P, 2, RBS * 3, B_K])
            vc = a.sb("b_vc", [P, CBS, ROWS, KC])
        flat = scratch[:, :, :].rearrange("p t d -> p (t d)")
        pt_flat = flat[:, 0:2 * HT * W].rearrange("p (h x) -> p h x", h=2)
        pt = pt_flat.rearrange("p h (t c q) -> p h t c q", t=HT, c=NC)
        vt = flat[:, TT * D // 2:TT * D // 2 + NV * P].rearrange("p (v f) -> p v f", v=NV)
        pj = a.ps(tag + "_pj", [P, 2, NB])
        sc = a.ps(tag + "_sc", [P, 2, NB])
        tr = a.ps(tag + "_tr", [P, 2, NB])
        o = a.ps(tag + "_o", [P, 2, NB])
        block = st.enter_context(nc.Block())
        w_v = w_in.rearrange("(k p) n -> p k n", p=P)

        def over_pairs(engine, pair):
            pair(0, True, False)
            with engine.Fori(1, HP - 1) as p:
                pair(p, False, False)
            pair(HP - 1, False, True)

        @block.sync
        def _(sp):
            def load_weights(p, first):
                if not first:
                    sp.wait_ge(w_lo, p)
                for j in range(3):
                    sp.dma_start(raw[:, :, j, :], w_v[:, :, bass.ds(p * P + (w_at + j * D // 2), P)]
                                 ).then_inc(w_ld, 16)

            def pair(p, first, last):
                if not last:
                    load_weights(p + 1, False)
                if dil:
                    if not first:
                        sp.wait_ge(low, NU * p)
                    sp.dma_start(bias[:, :], bias_in[:, bass.ds(p, 1), :].rearrange("p o w -> p (o w)")
                                 ).then_inc(b_ld, 16)
                sp.wait_ge(y_out, HALVES * (p + 1))
                sp.dma_start(y_t[bass.ds(p + y_at, 1)].rearrange("o p s -> (o p) s"), y[:, :]
                             ).then_inc(y_st, 16)

            load_weights(0, True)
            if not dil:
                sp.dma_start(mask[:, :, :], bias_in).then_inc(b_ld, 16)
            over_pairs(sp, pair)
            sp.wait_ge(y_st, 16 * HP)

        @block.gpsimd
        def _(pool):
            for i in range(2):
                nc.gpsimd.memset(q[HD * (1 - i):HD * (2 - i), i, :], 0.0).then_inc(zeroed, 1)
            if dil:
                return
            pool.wait_ge(zeroed, 2)
            for p in range(HP):
                if p >= 1:
                    pool.wait_ge(b_ready, 2 * RBS * 3 * p)
                for rr in range(QR):
                    at = (QR - 1 - rr) * TAB_W
                    pool.dma_start(runs[QC * rr:QC * rr + QC, :, 0:RUN],
                                   tab[:, 2 * p:2 * p + 2, at:at + RUN]).then_inc(r_ld, 16)
                pool.wait_ge(r_ld, 16 * QR * (p + 1))
                if p == 0:
                    pool.wait_ge(b_ld, 16)
                else:
                    pool.wait_ge(low, NU * p)
                for i in range(2):
                    for rb in range(RBS):
                        for kind in range(3):
                            r0, c0 = 4 - 4 * rb, QC - 8 * kind
                            run = runs[:, i, :].rearrange("p (r w) -> p r w", w=TAB_W)[
                                :, r0:r0 + KR, c0:c0 + KC]
                            m = mask[:, rb * 3 + kind].rearrange("p (r w) -> p r w", w=KC)
                            b = bias[:, i, rb * 3 + kind].rearrange("p (r w) -> p r w", w=KC)
                            nc.gpsimd.tensor_tensor(b, run, m, ALU.add).then_inc(b_ready, 1)

        @block.scalar
        def _(act):
            def split(p, first):
                act.wait_ge(w_ld, 48 * (p + 1))
                if not first:
                    act.wait_ge(pj_mm, NPJ * p)
                nc.scalar.copy(wh[:, :, :, :], raw[:, :, :, :]).then_inc(w_hi, 1)

            def exponential(p, m, first):
                u, b = NU * p + m, m % 2
                act.wait_ge(low, u + 1)
                if not (first and m < 2):
                    act.wait_ge(divided, u - 1)
                nc.scalar.activation(ex[:, b, :], t_s[:, b, :], ACT.Exp, bias=sm[:, b, 0:1], scale=-1.0,
                                     accum_out=sm[:, b, 1:2]).then_inc(exped, 1)

            def turned_out(p, m, first):
                act.wait_ge(p_tr, NU * p + m + 1)
                half, n = m // UN, m % UN
                if n == 0 and not (first and half == 0):
                    act.wait_ge(pv, HALVES * p + half)
                nc.scalar.copy(pt[:, n % 2, n // 2], tr[:, n % 2, 0:W].rearrange("p (c q) -> p c q", c=NC)
                               ).then_inc(p_out, 1)

            def pair(p, first, last):
                for m in range(NU + LAG):
                    if m < NU:
                        exponential(p, m, first)
                    if m >= LAG:
                        turned_out(p, m - LAG, first)
                    if m == UN and not last:
                        split(p + 1, False)

            split(0, True)
            over_pairs(act, pair)

        @block.vector
        def _(dve):
            def split(p):
                dve.wait_ge(w_hi, p + 1)
                nc.vector.tensor_tensor(wl[:, :, :, :], raw[:, :, :, :], wh[:, :, :, :].bitcast(F32),
                                        ALU.subtract).then_inc(w_lo, 1)

            def project(p):
                for j in range(3):
                    for half in range(HALVES):
                        cols = slice(NB * half, NB * half + NB)
                        src = pj[:, half, :]
                        dve.wait_ge(pj_mm, NPJ * p + 2 * j + half + 1)
                        if j == 0:
                            for i in range(2):
                                rows = slice(HD * i, HD * i + HD)
                                if dil:
                                    to = q[rows, i, cols].rearrange("p (t r m) -> p t r m", r=CL, m=CQ)
                                    of = pj[rows, half, :].rearrange("p (t m r) -> p t r m", r=CL, m=CQ)
                                else:
                                    to = q[rows, i, :].rearrange("p (c b r w) -> p c b r w", c=CBS, b=RBS,
                                                                 r=QR)[:, :, half]
                                    of = pj[rows, half, :].rearrange("p (r c w) -> p c r w", r=QR, c=CBS)
                                ins = nc.vector.tensor_scalar(to, of, -HD ** -0.5, None, ALU.mult)
                        else:
                            if j == 1 and dil:
                                m0 = CK // HALVES * half
                                nc.vector.tensor_copy(kc[:, :, m0:m0 + CK // HALVES],
                                                      src.rearrange("p (m r) -> p r m", r=CL))
                            if j == 2 and not dil:
                                for cb in range(CBS):
                                    ins = nc.vector.tensor_copy(
                                        vc[:, cb, QR * half:QR * half + QR, :],
                                        src.rearrange("p (r c) -> p r c", c=COLS)[:, :, KC0[cb]:KC0[cb] + KC])
                                ins.then_inc(pj_out, 1)
                                continue
                            ins = nc.vector.tensor_copy(kv[:, j - 1, cols], src)
                        ins.then_inc(pj_out, 1)

            def values(p):
                for g in range(NVG):
                    n = min(VB, NV - VB * g)
                    dve.wait_ge(v_tr, NVG * p + g + 1)
                    nc.vector.tensor_copy(vt[:, VB * g:VB * g + n, :],
                                          tr[:, g % 2, 0:P * n].rearrange("p (v f) -> p v f", v=n)
                                          ).then_inc(v_out, 1)

            def tile_bias(m):
                t, i = m // 2, m % 2
                if dil:
                    band = band_start(t) - P * t + P
                    at = A_W * i + band
                    step = BAND_W + (CK - CQ) - CQ * t - band
                    return bias[:, at:at + 2 * step].rearrange("p (a s) -> p a s", s=step)[:, :, 0:BAND]
                cb, rb = t // RBS, t % RBS
                return bias[:, i, rb * 3 + KIND[cb]]

            def step(p, m, first):
                u, b = NU * p + m, m % 2
                if m < NU:
                    dve.wait_ge(qk, u + 1)
                if m == 0 and dil:
                    dve.wait_ge(b_ld, 16 * (p + 1))
                if m == 0 and not dil:
                    dve.wait_ge(b_ready, 2 * RBS * 3 * (p + 1))
                if not (first and m < 2):
                    dve.wait_ge(exped, u - 1)
                if m < 2:
                    nc.vector.memset(sm[:, b, 3:4], 0.0)
                else:
                    nc.vector.reciprocal(sm[:, b, 2:3], sm[:, b, 1:2]).then_inc(rec, 1)
                if m < NU:
                    of, to = sc[:, b, 0:W], t_s[:, b, :]
                    if dil:
                        of, to = (x.rearrange("p (a k) -> p a k", a=2) for x in (of, to))
                    nc.vector.tensor_tensor_reduce(to, of, tile_bias(m), 1.0, 3e38, ALU.add, ALU.min,
                                                   sm[:, b, 0:1]).then_inc(low, 1)
                if m < 2:
                    return
                dve.wait_ge(rec, u - 1)
                if not (first and m < 4):
                    dve.wait_ge(p_tr, u - 3)
                nc.vector.tensor_scalar(pn[:, b, :], ex[:, b, :], sm[:, b, 2:3], None,
                                        ALU.mult).then_inc(divided, 1)

            def output(p, half, first):
                dve.wait_ge(pv, HALVES * p + half + 1)
                if half == 0 and not first:
                    dve.wait_ge(y_st, 16 * p)
                if dil:
                    to = y[:, NB * half:NB * half + NB].rearrange("p (t m r) -> p t r m", r=CL, m=CQ)
                    of = o[:, half, :].rearrange("p (t r m) -> p t r m", r=CL, m=CQ)
                    ins = nc.vector.tensor_copy(to, of)
                else:
                    n = CBS // HALVES
                    to = y[:, :].rearrange("p (b r c w) -> p b r c w", b=RBS, r=QR, c=CBS)
                    of = o[:, half, :].rearrange("p (c b r w) -> p c b r w", c=n, b=RBS, r=QR)
                    for c in range(n):
                        for b in range(RBS):
                            ins = nc.vector.tensor_copy(to[:, b, :, n * half + c], of[:, c, b])
                ins.then_inc(y_out, 1)

            def pair(p, first, last):
                project(p)
                values(p)
                for m in range(NU + 2):
                    step(p, m, first)
                    if m == UN + LAG + 2:
                        output(p, 0, first)
                        if not last:
                            split(p + 1)
                output(p, 1, first)

            split(0)
            over_pairs(dve, pair)

        @block.tensor
        def _(pe):
            def project(p, first):
                pe.wait_ge(w_lo, p + 1)
                for j in range(3):
                    for half in range(HALVES):
                        x = 2 * j + half
                        if not (first and j == 0):
                            pe.wait_ge(pj_out, NPJ * p + x - 1)
                        for k in range(KT):
                            for n, (l, r) in enumerate(((wh, ut_hi), (wh, ut_lo), (wl, ut_hi))):
                                last = nc.tensor.matmul(pj[:, half, :], l[:, k, j, :],
                                                        r[:, k, NB * half:NB * half + NB],
                                                        start=(k == 0 and n == 0),
                                                        stop=(k == KT - 1 and n == 2))
                        last.then_inc(pj_mm, 1)

            def value_source(v):
                if dil:
                    start, step = value_tiles_a()[v]
                    return kv[:, 1, start:start + step * (P - 1) + 1:step]
                rc, cb = v // CBS, v % CBS
                return vc[:, cb, RC * rc:RC * rc + RC, :].rearrange("p r c -> p (r c)")

            def values(p, first):
                pe.wait_ge(pj_out, NPJ * (p + 1))
                if not first:
                    pe.wait_ge(p_out, NU * p)
                for g in range(NVG):
                    if g >= 2:
                        pe.wait_ge(v_out, NVG * p + g - 1)
                    for v in range(VB * g, min(VB * g + VB, NV)):
                        at = P * (v - VB * g)
                        last = nc.tensor.transpose(tr[:, g % 2, at:at + P], value_source(v), ident[:, :])
                    last.then_inc(v_tr, 1)

            def score(p, m, first):
                u, b = NU * p + m, m % 2
                t, i = m // 2, m % 2
                if not (first and m < 2):
                    pe.wait_ge(low, u - 1)
                if dil:
                    w0 = band_start(t)
                    nc.tensor.matmul(sc[:, b, 0:BAND], q[:, i, P * t:P * t + P], kv[:, 0, w0:w0 + BAND],
                                     start=True, stop=True, skip_group_check=True)
                    for r in range(CL):
                        last = nc.tensor.matmul(sc[CQ * r:CQ * r + CQ, b, BAND:BAND + CK],
                                                q[:, i, P * t + CQ * r:P * t + CQ * r + CQ], kc[:, r, :],
                                                start=True, stop=True, skip_group_check=True)
                else:
                    cb, rb = t // RBS, t % RBS
                    grid = kv[:, 0, :].rearrange("p (r c) -> p r c", c=COLS)
                    last = nc.tensor.matmul(sc[:, b, 0:W], q[:, i, P * t:P * t + P],
                                            grid[:, 4 * rb:4 * rb + KR, KC0[cb]:KC0[cb] + KC],
                                            start=True, stop=True)
                last.then_inc(qk, 1)

            def turn(p, m, first):
                u, b = NU * p + m, m % 2
                pe.wait_ge(divided, u + 1)
                if m < 2:
                    pe.wait_ge(v_out, NVG * (p + 1))
                else:
                    pe.wait_ge(p_out, u - 1)
                for c in range(NC):
                    last = nc.tensor.transpose(tr[:, b, P * c:P * c + P], pn[:, b, P * c:P * c + P],
                                               ident[:, :])
                last.then_inc(p_tr, 1)

            def multiply(p, half, first):
                pe.wait_ge(p_out, NU * p + UN * (half + 1))
                if not first:
                    pe.wait_ge(y_out, HALVES * (p - 1) + half + 1)
                todo = products(dil, half)
                for n, (v, users, cls) in enumerate(todo):
                    for i in range(2):
                        to = o[HD * i:HD * i + HD, half, :]
                        if cls is not None:
                            to = to.rearrange("p (t r m) -> p t r m", r=CL, m=CQ)[:, :, cls]
                            of = pt[:, i, :, users[0][1], CQ * cls:CQ * cls + CQ]
                        else:
                            t, ch = users[0]
                            to = to[:, P * t:P * (t + len(users))]
                            of = pt[:, i, t, ch]
                            if len(users) == 2:
                                at, step = (t * NC + ch) * P, (NC - 1) * P
                                of = pt_flat[:, i, at:at + 2 * step].rearrange(
                                    "p (a s) -> p a s", s=step)[:, :, 0:P]
                        last = nc.tensor.matmul(to, vt[:, v, HD * i:HD * i + HD], of, start=(n == 0),
                                                stop=(n == len(todo) - 1), skip_group_check=True)
                last.then_inc(pv, 1)

            def pair(p, first, last):
                project(p, first)
                values(p, first)
                for m in range(NU + LAG):
                    if m < NU:
                        score(p, m, first)
                    if m >= LAG:
                        turn(p, m - LAG, first)
                    if m - LAG == UN - 1:
                        multiply(p, 0, first)
                multiply(p, 1, first)

            pe.wait_ge(zeroed, 2)
            over_pairs(pe, pair)


def output_projection_phase(nc, top, w_out, y_t, ut_hi, ut_lo, acc):
    y_ld = [top.sem(f"o_y_ld{b}") for b in range(2)]
    w_ld = [top.sem(f"o_w_ld{b}") for b in range(2)]
    y_hi, y_lo, w_hi, w_lo = top.sem("o_y_hi"), top.sem("o_y_lo"), top.sem("o_w_hi"), top.sem("o_w_lo")
    mm, out = top.sem("o_mm"), top.sem("o_out")
    with ExitStack() as st:
        a = Parts(nc, st)
        y = a.sb("o_y", [P, 2, S])
        w = a.sb("o_w", [P, 2, D])
        wh = a.sb("o_wh", [P, KT, D], F32R)
        wl = a.sb("o_wl", [P, KT, D], F32R)
        ps = a.ps("o_ps", [P, 4, NB])
        block = st.enter_context(nc.Block())

        @block.sync
        def _(sp):
            for k in range(KT):
                b = k % 2
                if k >= 2:
                    sp.wait_ge(y_lo, k - 1)
                    sp.wait_ge(w_lo, k - 1)
                sp.dma_start(y[:, b, :], y_t[k]).then_inc(y_ld[b], 16)
                sp.dma_start(w[:, b, :], w_out[P * k:P * k + P, :]).then_inc(w_ld[b], 16)

        @block.scalar
        def _(act):
            for k in range(KT):
                act.wait_ge(y_ld[k % 2], 16 * (k // 2 + 1))
                nc.scalar.copy(ut_hi[:, k, :], y[:, k % 2, :]).then_inc(y_hi, 1)
                act.wait_ge(w_ld[k % 2], 16 * (k // 2 + 1))
                nc.scalar.copy(wh[:, k, :], w[:, k % 2, :]).then_inc(w_hi, 1)

        @block.vector
        def _(dve):
            for k in range(KT):
                dve.wait_ge(y_hi, k + 1)
                nc.vector.tensor_tensor(ut_lo[:, k, :], y[:, k % 2, :], ut_hi[:, k, :].bitcast(F32),
                                        ALU.subtract).then_inc(y_lo, 1)
                dve.wait_ge(w_hi, k + 1)
                nc.vector.tensor_tensor(wl[:, k, :], w[:, k % 2, :], wh[:, k, :].bitcast(F32),
                                        ALU.subtract).then_inc(w_lo, 1)
            for j in range(TT * HALVES):
                dve.wait_ge(mm, j + 1)
                nc.vector.tensor_copy(acc[:, j // 2, NB * (j % 2):NB * (j % 2) + NB],
                                      ps[:, j % 4, :]).then_inc(out, 1)

        @block.tensor
        def _(pe):
            pe.wait_ge(w_lo, KT)
            for j in range(TT * HALVES):
                t, half = j // 2, j % 2
                if j >= 4:
                    pe.wait_ge(out, j - 3)
                for k in range(KT):
                    for n, (l, r) in enumerate(((ut_hi, wh), (ut_hi, wl), (ut_lo, wh))):
                        last = nc.tensor.matmul(ps[:, j % 4, :], l[:, k, P * t:P * t + P],
                                                r[:, k, NB * half:NB * half + NB],
                                                start=(k == 0 and n == 0), stop=(k == KT - 1 and n == 2))
                last.then_inc(mm, 1)


def mixer(nc, top, w_in, rpb, w_out, a_bias, b_mask, tab, y_t, ident, ut_hi, ut_lo, acc):
    with nc.cleanup_on_exit():
        table_phase(nc, top, rpb, tab)
    with nc.cleanup_on_exit():
        attention_phase(nc, top, "a", w_in, 0, 0, ut_hi, ut_lo, acc, ident, a_bias, None, y_t)
    with nc.cleanup_on_exit():
        attention_phase(nc, top, "b", w_in, 3 * D // 2, HP, ut_hi, ut_lo, acc, ident, b_mask, tab, y_t)
    with nc.cleanup_on_exit():
        output_projection_phase(nc, top, w_out, y_t, ut_hi, ut_lo, acc)


def kernel_program(nc, x, c, w_ada, b_ada, g1, u1, d1, w_in, rpb, w_out, g2, u2, d2, ln_g, ln_b,
                   ident_in, a_bias, b_mask, out):
    mods_row = nc.dram_tensor("mods_row", [1, N_MOD * D], F32, kind="Internal").ap()
    mods = nc.dram_tensor("mods", [1, N_MOD * D], F32, kind="Internal").ap()
    h1 = nc.dram_tensor("h_after_ffn1", [S, D], F32, kind="Internal").ap()
    h2 = nc.dram_tensor("h_after_mix", [S, D], F32, kind="Internal").ap()
    y_t = nc.dram_tensor("mixed_turned", [KT, P, S], F32, kind="Internal").ap()
    tab = nc.dram_tensor("bias_table", [QC, HEADS, TAB_R * TAB_W], F32, kind="Internal").ap()
    with ExitStack() as st:
        top = Parts(nc, st)
        mod_col = top.sb("mod_col", [P, 3 * 2 * KT])
        ident = top.sb("ident", [P, P])
        with nc.cleanup_on_exit():
            modulation_phase(nc, top, c, w_ada, b_ada, ident_in, mods_row, mods, mod_col, ident)
        ut_hi = top.sb("ut_hi", [P, KT, S], F32R)
        ut_lo = top.sb("ut_lo", [P, KT, S], F32R)
        acc = top.sb("acc", [P, TT, D])

        def gate(j):
            return mods[:, (3 * j + 2) * D:(3 * j + 3) * D]

        def ln(a, j):
            return a[0, j:j + 1, :]

        with nc.cleanup_on_exit():
            boundary_phase(nc, top, "in", x, None, acc, None, None, None, 0.0, 0, mod_col, ident, ut_hi, ut_lo)
        with nc.cleanup_on_exit():
            ffn_phase(nc, top, "f1", g1, u1, d1, ut_hi, ut_lo, acc)
        with nc.cleanup_on_exit():
            boundary_phase(nc, top, "b1", x, h1, acc, gate(0), ln(ln_g, 0), ln(ln_b, 0), 0.5, 1,
                           mod_col, ident, ut_hi, ut_lo)
        mixer(nc, top, w_in, rpb, w_out, a_bias, b_mask, tab, y_t, ident, ut_hi, ut_lo, acc)
        with nc.cleanup_on_exit():
            boundary_phase(nc, top, "b2", h1, h2, acc, gate(1), ln(ln_g, 1), ln(ln_b, 1), 1.0, 2,
                           mod_col, ident, ut_hi, ut_lo)
        with nc.cleanup_on_exit():
            ffn_phase(nc, top, "f2", g2, u2, d2, ut_hi, ut_lo, acc)
        with nc.cleanup_on_exit():
            boundary_phase(nc, top, "b3", h2, out, acc, gate(2), ln(ln_g, 2), ln(ln_b, 2), 0.5, None,
                           mod_col, ident, ut_hi, ut_lo)


def kernel(x, c, w_ada, b_ada, ffn1_w_gate, ffn1_w_up, ffn1_w_down, w_in, rpb, w_out,
           ffn2_w_gate, ffn2_w_up, ffn2_w_down, ln_g, ln_b):
    import concourse.bacc as bacc
    from concourse.bass_utils import run_bass_kernel_spmd

    nc = bacc.Bacc("TRN2", target_bir_lowering=False, num_devices=1)
    arrays = dict(x=x, c=c, w_ada=w_ada, b_ada=b_ada, ffn1_w_gate=ffn1_w_gate, ffn1_w_up=ffn1_w_up,
                  ffn1_w_down=ffn1_w_down, w_in=w_in, rpb=rpb, w_out=w_out, ffn2_w_gate=ffn2_w_gate,
                  ffn2_w_up=ffn2_w_up, ffn2_w_down=ffn2_w_down, ln_g=ln_g, ln_b=ln_b)
    arrays.update(identity=np.eye(P, dtype=np.float32), dilated_bias=dilated_bias(),
                  window_masks=window_masks())
    arrays = {n: np.ascontiguousarray(v) for n, v in arrays.items()}
    d = {n: nc.dram_tensor("in_" + n, list(v.shape), F32, kind="ExternalInput").ap()
         for n, v in arrays.items()}
    out = nc.dram_tensor("out", [1, S, D], F32, kind="ExternalOutput").ap()
    kernel_program(nc, d["x"][0], d["c"], d["w_ada"], d["b_ada"], d["ffn1_w_gate"][0], d["ffn1_w_up"][0],
                   d["ffn1_w_down"][0], d["w_in"][0], d["rpb"], d["w_out"][0], d["ffn2_w_gate"][0],
                   d["ffn2_w_up"][0], d["ffn2_w_down"][0], d["ln_g"], d["ln_b"], d["identity"],
                   d["dilated_bias"], d["window_masks"], out[0])
    got = run_bass_kernel_spmd(nc, [{"in_" + n: v for n, v in arrays.items()}], core_ids=[0])
    return got.results[0]["out"]
```

```python
from contextlib import ExitStack

import concourse.bass as bass
import concourse.mybir as mybir
import numpy as np

F32 = mybir.dt.float32
F32R = mybir.dt.float32r
ALU = mybir.AluOpType
ACT = mybir.ActivationFunctionType
AX = mybir.AxisListType

P = 128
S = 1024
D = 1024
F = 2816
N_MOD = 9
KT = D // P
TT = S // P
NB = 512
HALVES = S // NB
FC = F // P
PAIRS = FC // 2
M_LATER = 22 * 256
M_FIRST = N_MOD * D - M_LATER
ALPHA = 2.0 ** 0.25
EPS = 1e-5
HD = 64
HEADS = 8
HP = HEADS // 2
BIG = 1e30

CL = 4
CQ = P // CL
CK = S // CL
BAND = 256
BAND_W = 384
CLS_W = CK + CK - CQ
A_W = BAND_W + CLS_W
A_PAD = 2 * A_W + 256
NAT = (0, 1, TT - 2, TT - 1)
OFFS = tuple(range(HD, S - P - HD + 1, P))
A_VT = len(NAT) + len(OFFS) + 2 * CL

ROWS, COLS = 16, 64
QR, QC = 8, 16
KH, KW = 8, 16
KR, KC = 12, 32
B_K = KR * KC
CBS = COLS // QC
RBS = ROWS // QR
RC = 4
TAB_R, TAB_W = 23, 64
RUN_R = 16
RUN = (RUN_R - 1) * TAB_W + 48
KC0 = tuple(min(max(QC * c - KW // 2, 0), COLS - KC) for c in range(CBS))
KIND = (0, 1, 1, 2)


def slopes():
    return 2.0 ** (-8.0 * np.arange(1, HEADS + 1) / HEADS)


def dilated_bias():
    q = np.arange(P)
    tok = 4 * (q % CQ) + q // CQ
    rel_band = np.arange(BAND_W)[None, :] - P - tok[:, None]
    rel_cls = np.arange(CLS_W)[None, :] - (CK - CQ) - (q % CQ)[:, None]
    count = (np.abs(rel_cls) <= 64).astype(np.float64) + (rel_cls % 4 == 0)
    out = np.zeros((P, HP, A_PAD), np.float32)
    for h, s in enumerate(slopes()):
        band = np.where(np.abs(rel_band) <= 64, s * np.abs(rel_band), BIG)
        cls = np.where(count > 0, s * 4 * np.abs(rel_cls) - np.log(np.maximum(count, 1)), BIG)
        at = (h % 2) * A_W
        out[:, h // 2, at:at + A_W] = np.concatenate([band, cls], axis=1)
    return out


def window_masks():
    out = np.zeros((P, RBS * 3, KR, KC), np.float32)
    for rb in range(RBS):
        for cb in range(CBS):
            for q in range(P):
                r, c = QR * rb + q // QC, QC * cb + q % QC
                r0 = min(max(r - KH // 2, 0), ROWS - KH)
                c0 = min(max(c - KW // 2, 0), COLS - KW)
                rows = 4 * rb + np.arange(KR)
                cols = KC0[cb] + np.arange(KC)
                ok = ((rows >= r0) & (rows < r0 + KH))[:, None] & ((cols >= c0) & (cols < c0 + KW))
                out[q, rb * 3 + KIND[cb]] = np.where(ok, 0.0, BIG)
    return out.reshape(P, RBS * 3, B_K)


class Parts:

    def __init__(self, nc, stack):
        self.nc, self.stack = nc, stack

    def sb(self, name, shape, dt=F32):
        return self.stack.enter_context(self.nc.sbuf_tensor(name, shape, dt))

    def ps(self, name, shape, dt=F32):
        return self.stack.enter_context(self.nc.psum_tensor(name, shape, dt))

    def sem(self, name):
        return self.nc.alloc_semaphore(name=name)


def modulation_phase(nc, top, c, w_ada, ident_in, rpb, mods_row, ident, cs, tab):
    n = 4
    cw = M_FIRST // n
    tw = cw // 4
    in_ld, w_ld = top.sem("m_in_ld"), [top.sem(f"m_w_ld{b}") for b in range(2)]
    c_ready, mm_done, row_done = top.sem("m_c_ready"), top.sem("m_mm"), top.sem("m_row")
    row_st, rpb_ld, tab_st = top.sem("m_row_st"), top.sem("m_rpb_ld"), top.sem("m_tab_st")
    zeroed, neg = top.sem("m_zeroed"), top.sem("m_neg")
    nr, nw = rpb.shape[2:]
    with ExitStack() as st:
        a = Parts(nc, st)
        w = a.sb("m_w", [P, 2, KT, cw])
        ccol = a.sb("m_c", [P, KT])
        row = a.sb("m_rowbuf", [1, M_FIRST])
        raw = a.sb("m_raw", [HEADS, nr, nw])
        pad = a.sb("m_pad", [HEADS, TAB_R, TAB_W])
        acc = a.ps("m_acc", [P, 2, NB])
        block = st.enter_context(nc.Block())

        @block.sync
        def _(sp):
            with nc.allow_non_contiguous_dma(reason="one short vector"):
                sp.dma_start(ccol[:, :], c.rearrange("o (k p) -> p (o k)", p=P)).then_inc(in_ld, 16)
            for i in range(n):
                if i >= 2:
                    sp.wait_ge(mm_done, i - 1)
                sp.dma_start(w[:, i % 2], w_ada[:, :, cw * i:cw * i + cw]).then_inc(w_ld[i % 2], 16)
            sp.wait_ge(row_done, 4 * n)
            sp.dma_start(mods_row[:, 0:M_FIRST], row[:, :]).then_inc(row_st, 16)
            sp.wait_ge(row_st, 16)

        @block.scalar
        def _(act):
            act.dma_start(ident[:, :], ident_in).then_inc(in_ld, 16)
            act.dma_start(raw[:, :, :], rpb[0]).then_inc(rpb_ld, 16)
            act.wait_ge(in_ld, 32)
            nc.scalar.activation(cs[:, :], ccol[:, :], ACT.Silu).then_inc(c_ready, 1)
            act.wait_ge(neg, 1)
            flat = pad[:, :, :].rearrange("h r w -> h (r w)")
            for m in range(QC):
                shift = QC - 1 - m
                act.dma_start(tab[m, :, 0:TAB_R * TAB_W - shift],
                              flat[:, shift:TAB_R * TAB_W]).then_inc(tab_st, 16)
            act.wait_ge(tab_st, 16 * QC)

        @block.tensor
        def _(pe):
            pe.wait_ge(c_ready, 1)
            for i in range(n):
                pe.wait_ge(w_ld[i % 2], 16 * (i // 2 + 1))
                if i >= 2:
                    pe.wait_ge(row_done, 4 * (i - 1))
                for k in range(KT):
                    for j in range(4):
                        last = nc.tensor.matmul(acc[32 * j:32 * j + 1, i % 2, 0:tw], cs[:, k:k + 1],
                                                w[:, i % 2, k, tw * j:tw * j + tw],
                                                start=(k == 0), stop=(k == KT - 1))
                last.then_inc(mm_done, 1)

        @block.vector
        def _(dve):
            nc.vector.memset(pad[:, :, :], 0.0).then_inc(zeroed, 1)
            dve.wait_ge(zeroed, 1)
            dve.wait_ge(rpb_ld, 16)
            r0, c0 = (TAB_R - nr) // 2, (TAB_W - 1 - nw) // 2
            nc.vector.tensor_scalar(pad[:, r0:r0 + nr, c0:c0 + nw], raw[:, :, :], -1.0, None,
                                    ALU.mult).then_inc(neg, 1)
            for i in range(n):
                dve.wait_ge(mm_done, i + 1)
                for j in range(4):
                    at = cw * i + tw * j
                    nc.vector.tensor_copy(row[0:1, at:at + tw],
                                          acc[32 * j:32 * j + 1, i % 2, 0:tw]).then_inc(row_done, 1)


def columns_phase(nc, top, tag, first, n, mods_row, b_ada, mods, mod_col, ident):
    rows = 3 * KT * n
    at = 3 * KT * first * P
    ld, summed, turned_s, done, stored = (top.sem(f"{tag}_{x}") for x in ("ld", "sum", "tr", "col", "st"))
    with ExitStack() as st:
        a = Parts(nc, st)
        grid = a.sb(tag + "_grid", [rows, P])
        bgrid = a.sb(tag + "_bgrid", [rows, P])
        sums = a.sb(tag + "_sums", [rows, P])
        turned = a.ps(tag + "_turned", [P, NB])
        block = st.enter_context(nc.Block())

        def as_rows(x):
            return x[:, at:at + rows * P].rearrange("o (r p) -> (o r) p", p=P)

        @block.sync
        def _(sp):
            sp.dma_start(grid[:, :], as_rows(mods_row)).then_inc(ld, 16)
            sp.dma_start(bgrid[:, :], as_rows(b_ada)).then_inc(ld, 16)
            sp.wait_ge(summed, 1)
            sp.dma_start(as_rows(mods), sums[:, :]).then_inc(stored, 16)
            sp.wait_ge(stored, 16)

        @block.tensor
        def _(pe):
            pe.wait_ge(summed, 1)
            nc.tensor.transpose(turned[:, 0:rows], sums[:, :], ident[0:rows, 0:rows]).then_inc(turned_s, 1)

        @block.vector
        def _(dve):
            dve.wait_ge(ld, 32)
            nc.vector.tensor_tensor(sums[:, :], grid[:, :], bgrid[:, :], ALU.add).then_inc(summed, 1)
            dve.wait_ge(turned_s, 1)
            src = turned[:, 0:rows].rearrange("p (j w k) -> p j w k", j=n, w=3)
            dst = mod_col[:, :].rearrange("p (j w k) -> p j w k", j=3, w=2)
            for j in range(n):
                nc.vector.tensor_copy(dst[:, first + j, 0], src[:, j, 0]).then_inc(done, 1)
                nc.vector.tensor_scalar(dst[:, first + j, 1], src[:, j, 1], 1.0, None, ALU.add).then_inc(done, 1)


def boundary_phase(nc, top, tag, acc, mod_col, ident, ut_hi, ut_lo, x=None, lng=None, lnb=None,
                   enter=None, store=None, prefetch=None):
    leave = lng is not None
    LAGB = 2 if leave else 0
    RING = 3

    def sem(name):
        return top.sem(f"{tag}_{name}")

    x_ld, bc_ld, stored = [sem(f"x_ld{b}") for b in range(RING)], sem("bc_ld"), [sem(f"st{b}") for b in range(RING)]
    eps_set, small = sem("eps_set"), sem("small")
    var_s, std_s, coef_s = ([sem(f"{n}{i}") for i in range(2)] for n in ("var", "std", "coef"))
    z_norm, gained, shifted, scaled = sem("z_norm"), sem("gained"), sem("shifted"), sem("scaled")
    n_done, tr_done, mod_done, hi_done, lo_done = sem("n"), sem("tr"), sem("mod"), sem("hi"), sem("lo")
    G = TT // HALVES
    with ExitStack() as st:
        a = Parts(nc, st)
        hn = a.sb(tag + "_hn", [P, RING, D])
        nrm = a.sb(tag + "_nrm", [P, TT, D])
        mod = a.sb(tag + "_mod", [P, 2, NB])
        rows = a.sb(tag + "_rows", [P, 2, D])
        sm = a.sb(tag + "_sm", [P, TT, 2, 20])
        eps = a.sb(tag + "_eps", [P, 1])
        turned = a.ps(tag + "_turned", [P, 2, NB])
        block = st.enter_context(nc.Block())

        def h_tile(t):
            return hn[:, t % RING, :]

        def ring_free(eng, t):
            if t < RING:
                return
            if enter is not None:
                eng.wait_ge(n_done, t - RING + 1)
                eng.wait_ge(scaled, t - RING + 1)
            else:
                eng.wait_ge(stored[t % RING], 16 * (t // RING))

        @block.sync
        def _(sp):
            if leave:
                for i, r in enumerate((lng, lnb)):
                    sp.dma_start(rows[:, i, :], r.broadcast_to([P, D])).then_inc(bc_ld, 16)
            waits = []
            for t in range(TT):
                if x is not None:
                    ring_free(sp, t)
                    sp.dma_start(h_tile(t), x[P * t:P * t + P, :]).then_inc(x_ld[t % RING], 16)
                if t == RING - 1 and prefetch is not None:
                    waits = prefetch(sp)
            if store is not None:
                for t in range(TT):
                    if enter is not None:
                        sp.wait_ge(scaled, t + 1)
                        sp.dma_start(store[P * t:P * t + P, :], acc[:, t, :]).then_inc(stored[t % RING], 16)
                    else:
                        sp.wait_ge(shifted, t + 1)
                        sp.dma_start(store[P * t:P * t + P, :], h_tile(t)).then_inc(stored[t % RING], 16)
                for b in range(RING):
                    sp.wait_ge(stored[b], 16 * len(range(b, TT, RING)))
            for s_, n in waits:
                sp.wait_ge(s_, n)

        @block.gpsimd
        def _(pool):
            if leave:
                pool.wait_ge(bc_ld, 32)
            for t in range(TT + LAGB):
                if leave and t < TT:
                    pool.wait_ge(z_norm, t + 1)
                    nc.gpsimd.tensor_tensor(h_tile(t), h_tile(t), rows[:, 0, :], ALU.mult).then_inc(gained, 1)
                if enter is not None and t >= LAGB:
                    if leave:
                        pool.wait_ge(shifted, t - LAGB + 1)
                    else:
                        pool.wait_ge(x_ld[t % RING], 16 * (t // RING + 1))
                    nc.gpsimd.tensor_scalar(acc[:, t - LAGB, :], h_tile(t - LAGB), ALPHA, 1.0, ALU.mult,
                                            ALU.mult).then_inc(scaled, 1)

        @block.scalar
        def _(act):
            act.wait_ge(eps_set, 1)

            def root(t, ln):
                act.wait_ge(var_s[ln], t + 1)
                nc.scalar.activation(sm[:, t, ln, 14:15], sm[:, t, ln, 13:14], ACT.Sqrt,
                                     bias=eps[:, 0:1]).then_inc(std_s[ln], 1)

            def normalise(to, of, t, ln, done):
                act.wait_ge(coef_s[ln], t + 1)
                nc.scalar.activation(to, of, ACT.Identity, bias=sm[:, t, ln, 19:20],
                                     scale=sm[:, t, ln, 18:19]).then_inc(done, 1)

            for t in range(TT + LAGB):
                e = t - LAGB
                if leave and t < TT:
                    root(t, 0)
                if enter is not None and e >= 0:
                    root(e, 1)
                if leave and t < TT:
                    ring_free(act, t)
                    normalise(h_tile(t), acc[:, t, :], t, 0, z_norm)
                if enter is not None and e >= 0:
                    normalise(nrm[:, e, :], h_tile(e), e, 1, n_done)
                    if e >= G:
                        evacuated = range(2 * (e - G), 2 * (e - G) + 2)
                        for y in list(evacuated) + (list(range(KT, 2 * KT)) if e == TT - 1 else []):
                            act.wait_ge(mod_done, y + 1)
                            nc.scalar.copy(ut_hi[:, y % KT, NB * (y // KT):NB * (y // KT) + NB],
                                           mod[:, y % 2, :]).then_inc(hi_done, 1)

        @block.tensor
        def _(pe):
            if enter is not None:
                for y in range(2 * KT):
                    pe.wait_ge(n_done, G * (y // KT + 1))
                    if y >= 2:
                        pe.wait_ge(mod_done, y - 1)
                    for g in range(G):
                        last = nc.tensor.transpose(turned[:, y % 2, P * g:P * g + P],
                                                   nrm[:, G * (y // KT) + g, P * (y % KT):P * (y % KT) + P],
                                                   ident[:, :])
                    last.then_inc(tr_done, 1)

        @block.vector
        def _(dve):
            count = [0]

            def chained(ins):
                count[0] += 1
                ins.then_inc(small, 1)
                dve.wait_ge(small, count[0])

            def statistics(of, t, ln):
                s_ = sm[:, t, ln, :]
                nc.vector.bn_stats(s_[:, 0:6], of[:, 0:NB])
                chained(nc.vector.bn_stats(s_[:, 6:12], of[:, NB:D]))
                nc.vector.bn_aggr(s_[:, 12:14], s_[:, 0:12]).then_inc(var_s[ln], 1)

            def coefficients(t, ln):
                s_ = sm[:, t, ln, :]
                mean, var, std, y_, a_, b_, r, nb = (s_[:, i:i + 1] for i in range(12, 20))
                dve.wait_ge(std_s[ln], t + 1)
                chained(nc.vector.reciprocal(y_, std))
                chained(nc.vector.tensor_scalar(a_, var, EPS, y_, ALU.add, ALU.mult))
                chained(nc.vector.tensor_scalar(b_, a_, y_, -0.5, ALU.mult, ALU.mult))
                chained(nc.vector.tensor_scalar(r, b_, 1.5, y_, ALU.add, ALU.mult))
                nc.vector.tensor_scalar(nb, mean, r, -1.0, ALU.mult, ALU.mult).then_inc(coef_s[ln], 1)

            def evacuate(y):
                dve.wait_ge(tr_done, y + 1)
                if y >= 2:
                    dve.wait_ge(lo_done, y - 1)
                m = 16 * enter + y % KT
                nc.vector.tensor_scalar(mod[:, y % 2, :], turned[:, y % 2, :], mod_col[:, m + 8:m + 9],
                                        mod_col[:, m:m + 1], ALU.mult, ALU.add).then_inc(mod_done, 1)

            def split(y):
                dve.wait_ge(hi_done, y + 1)
                cols = slice(NB * (y // KT), NB * (y // KT) + NB)
                nc.vector.tensor_tensor(ut_lo[:, y % KT, cols], mod[:, y % 2, :],
                                        ut_hi[:, y % KT, cols].bitcast(F32), ALU.subtract).then_inc(lo_done, 1)

            nc.vector.memset(eps[:, :], EPS).then_inc(eps_set, 1)
            if leave:
                dve.wait_ge(bc_ld, 32)
            for t in range(TT + LAGB):
                e = t - LAGB
                if leave and t < TT:
                    statistics(acc[:, t, :], t, 0)
                if e >= 0:
                    if leave:
                        dve.wait_ge(gained, e + 1)
                        nc.vector.tensor_tensor(h_tile(e), h_tile(e), rows[:, 1, :], ALU.add).then_inc(shifted, 1)
                        dve.wait_ge(shifted, e + 1)
                    else:
                        dve.wait_ge(x_ld[e % RING], 16 * (e // RING + 1))
                    if enter is not None:
                        statistics(h_tile(e), e, 1)
                if leave and t < TT:
                    coefficients(t, 0)
                if enter is not None and e >= 0:
                    coefficients(e, 1)
                    if e >= G:
                        todo = list(range(2 * (e - G), 2 * (e - G) + 2))
                        todo += list(range(KT, 2 * KT)) if e == TT - 1 else []
                        for n, y in enumerate(todo):
                            evacuate(y)
                            if n >= 1:
                                split(y - 1)
                        split(todo[-1])


def ffn_views(w_gate, w_up, w_down):
    return (w_gate.rearrange("(k p) n -> p k n", p=P), w_up.rearrange("(k p) n -> p k n", p=P),
            w_down.rearrange("(f p) n -> p f n", p=P))


def ffn_prefetch(views, raw, raw_d, loaded):
    def prefetch(sp):
        gate_v, up_v, down_v = views
        sp.dma_start(raw[:, :, 0, :], gate_v[:, :, 0:2 * P]).then_inc(loaded, 16)
        sp.dma_start(raw[:, :, 1, :], up_v[:, :, 0:2 * P]).then_inc(loaded, 16)
        sp.dma_start(raw_d[:, :, :], down_v[:, 0:2, :]).then_inc(loaded, 16)
        return [(loaded, 48)]
    return prefetch


def ffn_phase(nc, top, tag, views, raw, raw_d, gate, resid, ut_hi, ut_lo, acc, ada=None):
    ld_gu, ld_d = top.sem(tag + "_ld_gu"), top.sem(tag + "_ld_d")
    w_hi, w_lo = [top.sem(f"{tag}_w_hi{i}") for i in range(2)], [top.sem(f"{tag}_w_lo{i}") for i in range(2)]
    d_hi, d_lo = top.sem(tag + "_d_hi"), top.sem(tag + "_d_lo")
    gu_mm, silu_done, mul_done = top.sem(tag + "_gu_mm"), top.sem(tag + "_silu"), top.sem(tag + "_mul")
    hid_hi_s, hid_lo_s = top.sem(tag + "_hid_hi"), top.sem(tag + "_hid_lo")
    d_mm, d_add = top.sem(tag + "_d_mm"), top.sem(tag + "_d_add")
    g_ld, g_half, scaled = top.sem(tag + "_g_ld"), top.sem(tag + "_g_half"), top.sem(tag + "_scaled")
    NT = TT * HALVES
    DB = 4 if ada is None else 3
    AW = 256
    if ada is not None:
        cs, w_ada, mods_row = ada
        a_ld, a_mm, a_part = top.sem(tag + "_a_ld"), top.sem(tag + "_a_mm"), top.sem(tag + "_a_part")
        a_row, a_st = top.sem(tag + "_a_row"), top.sem(tag + "_a_st")
    gate_v, up_v, down_v = views
    with ExitStack() as st:
        a = Parts(nc, st)
        gates = a.sb(tag + "_gates", [P, D])
        wh = a.sb(tag + "_wh", [P, 2, KT, 2, P], F32R)
        wl = a.sb(tag + "_wl", [P, 2, KT, 2, P], F32R)
        dh = a.sb(tag + "_dh", [P, 2, D], F32R)
        dl = a.sb(tag + "_dl", [P, 2, D], F32R)
        hid_hi = a.sb(tag + "_hidh", [P, 2, S], F32R)
        hid_lo = a.sb(tag + "_hidl", [P, 2, S], F32R)
        sil = a.sb(tag + "_sil", [P, 2, NB])
        prod = a.sb(tag + "_prod", [P, 2, NB])
        gu = a.ps(tag + "_gu", [P, 2, 2, NB])
        dp = a.ps(tag + "_dp", [P, DB, NB])
        if ada is not None:
            aw = a.sb(tag + "_aw", [P, KT, AW])
            arow = a.sb(tag + "_arow", [1, 2, AW])
            am = a.ps(tag + "_am", [P, 2, AW])
        block = st.enter_context(nc.Block())

        @block.sync
        def _(sp):
            def load(q):
                sp.wait_ge(w_lo[1], q)
                cols = bass.ds(q * 2 * P, 2 * P)
                sp.dma_start(raw[:, :, 0, :], gate_v[:, :, cols]).then_inc(ld_gu, 16)
                sp.dma_start(raw[:, :, 1, :], up_v[:, :, cols]).then_inc(ld_gu, 16)
                sp.wait_ge(d_lo, q)
                sp.dma_start(raw_d[:, :, :], down_v[:, bass.ds(q * 2, 2), :]).then_inc(ld_d, 16)

            def store_row(q):
                if ada is not None:
                    sp.wait_ge(a_row, 2 * q + 2)
                    sp.dma_start(mods_row[:, bass.ds(q * 2 * AW + M_FIRST, 2 * AW)],
                                 arow[0:1, :, :].rearrange("p c n -> p (c n)")).then_inc(a_st, 16)

            sp.dma_start(gates[:, :], gate.broadcast_to([P, D])).then_inc(g_ld, 16)
            with sp.Fori(1, PAIRS) as q:
                load(q)
                store_row(q - 1)
            store_row(PAIRS - 1)
            if ada is not None:
                sp.wait_ge(a_st, 16 * PAIRS)

        @block.gpsimd
        def _(pool):
            def scale(q, first):
                if not first:
                    pool.wait_ge(ld_d, 16 * q)
                for i in range(2):
                    ins = nc.gpsimd.tensor_tensor(raw_d[:, i, :], raw_d[:, i, :], gates[:, :], ALU.mult)
                ins.then_inc(scaled, 1)

            def load_ada(q, i, first):
                if ada is not None:
                    if not first:
                        pool.wait_ge(a_mm, 2 * q + i)
                    pool.dma_start(aw[:, :, :], w_ada[:, :, bass.ds((q * 2 + i) * AW + M_FIRST, AW)]
                                   ).then_inc(a_ld, 16)

            pool.sem_inc(d_add, NT)
            load_ada(0, 0, True)
            pool.wait_ge(g_ld, 16)
            nc.gpsimd.tensor_scalar(gates[:, :], gates[:, :], resid, 1.0, ALU.mult, ALU.mult).then_inc(g_half, 1)
            pool.wait_ge(g_half, 1)
            scale(0, True)
            load_ada(0, 1, False)
            with pool.Fori(1, PAIRS) as q:
                load_ada(q, 0, False)
                scale(q, False)
                load_ada(q, 1, False)

        @block.scalar
        def _(act):
            def split_gu(q, i, first):
                if not first:
                    act.wait_ge(ld_gu, 32 * q)
                    act.wait_ge(gu_mm, 4 * q + 2 * i - 2)
                nc.scalar.copy(wh[:, i], raw[:, :, :, P * i:P * i + P]).then_inc(w_hi[i], 1)

            def split_d(q, first):
                act.wait_ge(scaled, q + 1)
                if not first:
                    act.wait_ge(d_mm, NT * q)
                nc.scalar.copy(dh[:, :, :], raw_d[:, :, :]).then_inc(d_hi, 1)

            def silu(q, i, first):
                for half in range(2):
                    s_ = 4 * q + 2 * i + half
                    act.wait_ge(gu_mm, s_ + 1)
                    if not first:
                        act.wait_ge(mul_done, s_ - 1)
                    nc.scalar.activation(sil[:, half, :], gu[:, half, 0, :],
                                         ACT.Silu).then_inc(silu_done, 1)

            def split_hid(q, i, first):
                for half in range(2):
                    s_ = 4 * q + 2 * i + half
                    act.wait_ge(mul_done, s_ + 1)
                    if not first:
                        act.wait_ge(d_mm, NT * q)
                    nc.scalar.copy(hid_hi[:, i, NB * half:NB * half + NB],
                                   prod[:, half, :]).then_inc(hid_hi_s, 1)

            def body(q, ahead):
                silu(q, 0, False)
                if ahead:
                    split_gu(q + 1, 0, False)
                split_hid(q, 0, False)
                split_d(q, False)
                silu(q, 1, False)
                split_hid(q, 1, False)
                if ahead:
                    split_gu(q + 1, 1, False)

            for i in range(2):
                split_gu(0, i, True)
            silu(0, 0, True)
            split_gu(1, 0, False)
            split_hid(0, 0, True)
            split_d(0, True)
            silu(0, 1, False)
            split_hid(0, 1, True)
            split_gu(1, 1, False)
            with act.Fori(1, PAIRS - 1) as q:
                body(q, True)
            body(PAIRS - 1, False)

        @block.vector
        def _(dve):
            def split_gu(q, i):
                dve.wait_ge(w_hi[i], q + 1)
                nc.vector.tensor_tensor(wl[:, i], raw[:, :, :, P * i:P * i + P], wh[:, i].bitcast(F32),
                                        ALU.subtract).then_inc(w_lo[i], 1)

            def split_d(q):
                dve.wait_ge(d_hi, q + 1)
                nc.vector.tensor_tensor(dl[:, :, :], raw_d[:, :, :], dh[:, :, :].bitcast(F32),
                                        ALU.subtract).then_inc(d_lo, 1)

            def mul(q, i, first):
                for half in range(2):
                    s_ = 4 * q + 2 * i + half
                    dve.wait_ge(silu_done, s_ + 1)
                    if not first:
                        dve.wait_ge(hid_lo_s, s_ - 1)
                    nc.vector.tensor_tensor(prod[:, half, :], sil[:, half, :], gu[:, half, 1, :],
                                            ALU.mult).then_inc(mul_done, 1)

            def split_hid(q, i):
                for half in range(2):
                    s_ = 4 * q + 2 * i + half
                    cols = slice(NB * half, NB * half + NB)
                    dve.wait_ge(hid_hi_s, s_ + 1)
                    nc.vector.tensor_tensor(hid_lo[:, i, cols], prod[:, half, :],
                                            hid_hi[:, i, cols].bitcast(F32),
                                            ALU.subtract).then_inc(hid_lo_s, 1)

            def add_down(q):
                for j in range(NT):
                    t, half = j // 2, j % 2
                    cols = slice(NB * half, NB * half + NB)
                    dve.wait_ge(d_mm, NT * q + j + 1)
                    dve.wait_ge(d_add, NT * q + j + 1)
                    nc.vector.tensor_tensor(acc[:, t, cols], dp[:, j % DB, :], acc[:, t, cols],
                                            ALU.add).then_inc(d_add, 1)

            def modulation(q, i, first):
                if ada is None:
                    return
                dve.wait_ge(a_mm, 2 * q + i + 1)
                if not first:
                    dve.wait_ge(a_st, 16 * q)
                nc.vector.tensor_copy(arow[0:1, i, :], am[0:1, i, :]).then_inc(a_part, 1)
                for j in range(1, 4):
                    dve.wait_ge(a_part, 6 * q + 3 * i + j)
                    nc.vector.tensor_tensor(arow[0:1, i, :], am[32 * j:32 * j + 1, i, :], arow[0:1, i, :],
                                            ALU.add).then_inc(a_part if j < 3 else a_row, 1)

            def body(q, ahead):
                mul(q, 0, False)
                add_down(q - 1)
                split_hid(q, 0)
                modulation(q, 0, False)
                split_d(q)
                if ahead:
                    split_gu(q + 1, 0)
                mul(q, 1, False)
                split_hid(q, 1)
                if ahead:
                    split_gu(q + 1, 1)
                modulation(q, 1, False)

            for i in range(2):
                split_gu(0, i)
            mul(0, 0, True)
            split_gu(1, 0)
            split_hid(0, 0)
            split_d(0)
            modulation(0, 0, True)
            mul(0, 1, False)
            split_hid(0, 1)
            split_gu(1, 1)
            modulation(0, 1, True)
            with dve.Fori(1, PAIRS - 1) as q:
                body(q, True)
            body(PAIRS - 1, False)
            add_down(PAIRS - 1)

        @block.tensor
        def _(pe):
            def gate_up(q, i, first):
                pe.wait_ge(w_lo[i], q + 1)
                for half in range(2):
                    s_ = 4 * q + 2 * i + half
                    cols = slice(NB * half, NB * half + NB)
                    if not first:
                        pe.wait_ge(mul_done, s_ - 1)
                    for g in range(2):
                        for k in range(KT):
                            for n, (l, r) in enumerate(((wh, ut_hi), (wh, ut_lo), (wl, ut_hi))):
                                last = nc.tensor.matmul(gu[:, half, g, :], l[:, i, k, g, :],
                                                        r[:, k, cols], start=(k == 0 and n == 0),
                                                        stop=(k == KT - 1 and n == 2))
                    last.then_inc(gu_mm, 1)

            def down(q, first=False):
                pe.wait_ge(hid_lo_s, 4 * (q + 1))
                pe.wait_ge(d_lo, q + 1)
                for j in range(NT):
                    t, half = j // 2, j % 2
                    pe.wait_ge(d_add, NT * (q + 1) + max(j - DB + 1, 0))
                    for i in range(2):
                        for n, (l, r) in enumerate(((hid_hi, dh), (hid_hi, dl), (hid_lo, dh))):
                            last = nc.tensor.matmul(dp[:, j % DB, :], l[:, i, P * t:P * t + P],
                                                    r[:, i, NB * half:NB * half + NB],
                                                    start=(i == 0 and n == 0), stop=(i == 1 and n == 2))
                    last.then_inc(d_mm, 1)

            def modulate(q, i, first):
                if ada is None:
                    return
                pe.wait_ge(a_ld, 32 * q + 16 * i + 16)
                if not first:
                    pe.wait_ge(a_row, 2 * q + i)
                for n in range(KT // 4):
                    for j in range(4):
                        k = KT // 4 * j + n
                        last = nc.tensor.matmul(am[32 * j:32 * j + 1, i, :], cs[:, k:k + 1], aw[:, k, :],
                                                start=(n == 0), stop=(n == KT // 4 - 1),
                                                skip_group_check=True)
                last.then_inc(a_mm, 1)

            gate_up(0, 0, True)
            modulate(0, 0, True)
            gate_up(0, 1, False)
            modulate(0, 1, False)
            with pe.Fori(1, PAIRS) as q:
                gate_up(q, 0, False)
                modulate(q, 0, False)
                down(q - 1)
                gate_up(q, 1, False)
                modulate(q, 1, False)
            down(PAIRS - 1)


def band_start(t):
    return min(max(P * t - HD, 0), S - BAND)


def value_tiles_a():
    return ([(P * n, 1) for n in NAT] + [(o, 1) for o in OFFS]
            + [(CL * P * c + r, CL) for r in range(CL) for c in range(2)])


def products(dil, half):
    out = []
    if not dil:
        for cb in range(CBS // HALVES):
            for rc in range(ROWS // RC):
                users = [(cb * RBS + rb, rc - rb) for rb in range(RBS) if 0 <= rc - rb < KR // RC]
                out.append((rc * CBS + half * CBS // HALVES + cb, users, None))
        return out
    for v, (start, step) in enumerate(value_tiles_a()):
        if step != 1:
            continue
        users = []
        for t in range(TT // HALVES):
            w0 = band_start(half * TT // HALVES + t)
            users += [(t, ch) for ch in range(BAND // P) if w0 + P * ch == start]
        if users:
            out.append((v, users, None))
    for r in range(CL):
        for c in range(CK // P):
            out.append((len(NAT) + len(OFFS) + 2 * r + c, [(t, BAND // P + c) for t in range(TT // HALVES)], r))
    return out


def attention_phase(nc, top, tag, w_in, w_at, y_at, ut_hi, ut_lo, scratch, ident, bias_in, tab, y_t):
    dil = tag == "a"
    NC = 4 if dil else 3
    W = NC * P
    HT = TT // HALVES
    NV = A_VT if dil else (ROWS // RC) * CBS
    VB = 4
    NVG = -(-NV // VB)
    UN = 2 * HT
    NU = HALVES * UN
    NPJ = 3 * HALVES
    LAG = 3
    PROJECTED = (2, 1, 0)

    def sem(name):
        return top.sem(f"{tag}_{name}")

    w_ld, b_ld, w_hi, w_lo = sem("w_ld"), sem("b_ld"), sem("w_hi"), sem("w_lo")
    zeroed, pj_mm, pj_out = sem("zeroed"), sem("pj_mm"), sem("pj_out")
    v_tr, v_out, qk, low, exped = sem("v_tr"), sem("v_out"), sem("qk"), sem("low"), sem("exped")
    rec, divided, p_tr, p_out = sem("rec"), sem("divided"), sem("p_tr"), sem("p_out")
    pv, y_out, y_st, b_ready, r_ld = sem("pv"), sem("y_out"), sem("y_st"), sem("b_ready"), sem("r_ld")
    with ExitStack() as st:
        a = Parts(nc, st)
        raw = a.sb(tag + "_raw", [P, KT, 3, P])
        wh = a.sb(tag + "_wh", [P, KT, 3, P], F32R)
        wl = a.sb(tag + "_wl", [P, KT, 3, P], F32R)
        q = a.sb(tag + "_q", [P, 2, S])
        kv = a.sb(tag + "_kv", [P, 2 if dil else 1, S])
        t_s = a.sb(tag + "_t", [P, 2, W])
        ex = a.sb(tag + "_ex", [P, 2, W])
        pn = a.sb(tag + "_pn", [P, 2, W])
        sm = a.sb(tag + "_sm", [P, 2, 4])
        y = a.sb(tag + "_y", [P, S])
        if dil:
            kc = a.sb("a_kc", [P, CL, CK])
            bias = a.sb("a_bias", [P, A_PAD])
        else:
            runs = a.sb("b_runs", [P, 2, RUN_R * TAB_W])
            mask = a.sb("b_mask", [P, RBS * 3, B_K])
            bias = a.sb("b_bias", [P, 2, RBS * 3, B_K])
            vc = a.sb("b_vc", [P, CBS, ROWS, KC])
        flat = scratch[:, :, :].rearrange("p t d -> p (t d)")
        pt_flat = flat[:, 0:2 * HT * W].rearrange("p (h x) -> p h x", h=2)
        pt = pt_flat.rearrange("p h (t c q) -> p h t c q", t=HT, c=NC)
        vt = flat[:, TT * D // 2:TT * D // 2 + NV * P].rearrange("p (v f) -> p v f", v=NV)
        pj = a.ps(tag + "_pj", [P, 2, NB])
        sc = a.ps(tag + "_sc", [P, 2, NB])
        tr = a.ps(tag + "_tr", [P, 2, NB])
        o = a.ps(tag + "_o", [P, 2, NB])
        block = st.enter_context(nc.Block())
        w_v = w_in.rearrange("(k p) n -> p k n", p=P)

        def over_pairs(engine, pair):
            pair(0, True, False)
            with engine.Fori(1, HP - 1) as p:
                pair(p, False, False)
            pair(HP - 1, False, True)

        @block.sync
        def _(sp):
            def load_weights(p, first):
                if not first:
                    sp.wait_ge(w_lo, p)
                for j in range(3):
                    sp.dma_start(raw[:, :, j, :], w_v[:, :, bass.ds(p * P + (w_at + j * D // 2), P)]
                                 ).then_inc(w_ld, 16)

            def pair(p, first, last):
                if not last:
                    load_weights(p + 1, False)
                if dil:
                    if not first:
                        sp.wait_ge(low, NU * p)
                    sp.dma_start(bias[:, :], bias_in[:, bass.ds(p, 1), :].rearrange("p o w -> p (o w)")
                                 ).then_inc(b_ld, 16)
                sp.wait_ge(y_out, HALVES * (p + 1))
                sp.dma_start(y_t[bass.ds(p + y_at, 1)].rearrange("o p s -> (o p) s"), y[:, :]
                             ).then_inc(y_st, 16)

            load_weights(0, True)
            if not dil:
                sp.dma_start(mask[:, :, :], bias_in).then_inc(b_ld, 16)
            over_pairs(sp, pair)
            sp.wait_ge(y_st, 16 * HP)

        @block.gpsimd
        def _(pool):
            for i in range(2):
                nc.gpsimd.memset(q[HD * (1 - i):HD * (2 - i), i, :], 0.0).then_inc(zeroed, 1)
            if dil:
                return
            pool.wait_ge(zeroed, 2)
            for p in range(HP):
                if p >= 1:
                    pool.wait_ge(b_ready, 2 * RBS * 3 * p)
                for rr in range(QR):
                    at = (QR - 1 - rr) * TAB_W
                    pool.dma_start(runs[QC * rr:QC * rr + QC, :, 0:RUN],
                                   tab[:, 2 * p:2 * p + 2, at:at + RUN]).then_inc(r_ld, 16)
                pool.wait_ge(r_ld, 16 * QR * (p + 1))
                if p == 0:
                    pool.wait_ge(b_ld, 16)
                else:
                    pool.wait_ge(low, NU * p)
                for i in range(2):
                    for rb in range(RBS):
                        for kind in range(3):
                            r0, c0 = 4 - 4 * rb, QC - 8 * kind
                            run = runs[:, i, :].rearrange("p (r w) -> p r w", w=TAB_W)[
                                :, r0:r0 + KR, c0:c0 + KC]
                            m = mask[:, rb * 3 + kind].rearrange("p (r w) -> p r w", w=KC)
                            b = bias[:, i, rb * 3 + kind].rearrange("p (r w) -> p r w", w=KC)
                            nc.gpsimd.tensor_tensor(b, run, m, ALU.add).then_inc(b_ready, 1)

        @block.scalar
        def _(act):
            def split(p, first):
                act.wait_ge(w_ld, 48 * (p + 1))
                if not first:
                    act.wait_ge(pj_mm, NPJ * p)
                nc.scalar.copy(wh[:, :, :, :], raw[:, :, :, :]).then_inc(w_hi, 1)

            def exponential(p, m, first):
                u, b = NU * p + m, m % 2
                act.wait_ge(low, u + 1)
                if not (first and m < 2):
                    act.wait_ge(divided, u - 1)
                nc.scalar.activation(ex[:, b, :], t_s[:, b, :], ACT.Exp, bias=sm[:, b, 0:1], scale=-1.0,
                                     accum_out=sm[:, b, 1:2]).then_inc(exped, 1)

            def turned_out(p, m, first):
                act.wait_ge(p_tr, NU * p + m + 1)
                half, n = m // UN, m % UN
                if n == 0 and not (first and half == 0):
                    act.wait_ge(pv, HALVES * p + half)
                nc.scalar.copy(pt[:, n % 2, n // 2], tr[:, n % 2, 0:W].rearrange("p (c q) -> p c q", c=NC)
                               ).then_inc(p_out, 1)

            def pair(p, first, last):
                for m in range(NU + LAG):
                    if m < NU:
                        exponential(p, m, first)
                    if m >= LAG:
                        turned_out(p, m - LAG, first)
                    if m == UN + LAG - 1 and not last:
                        split(p + 1, False)

            split(0, True)
            over_pairs(act, pair)

        @block.vector
        def _(dve):
            def split(p):
                dve.wait_ge(w_hi, p + 1)
                nc.vector.tensor_tensor(wl[:, :, :, :], raw[:, :, :, :], wh[:, :, :, :].bitcast(F32),
                                        ALU.subtract).then_inc(w_lo, 1)

            def project(p, j):
                for half in range(HALVES):
                    cols = slice(NB * half, NB * half + NB)
                    src = pj[:, half, :]
                    dve.wait_ge(pj_mm, NPJ * p + 2 * PROJECTED.index(j) + half + 1)
                    if j == 0:
                        for i in range(2):
                            rows = slice(HD * i, HD * i + HD)
                            if dil:
                                to = q[rows, i, cols].rearrange("p (t r m) -> p t r m", r=CL, m=CQ)
                                of = pj[rows, half, :].rearrange("p (t m r) -> p t r m", r=CL, m=CQ)
                            else:
                                to = q[rows, i, :].rearrange("p (c b r w) -> p c b r w", c=CBS, b=RBS,
                                                             r=QR)[:, :, half]
                                of = pj[rows, half, :].rearrange("p (r c w) -> p c r w", r=QR, c=CBS)
                            ins = nc.vector.tensor_scalar(to, of, -HD ** -0.5, None, ALU.mult)
                    elif j == 2 and not dil:
                        for cb in range(CBS):
                            ins = nc.vector.tensor_copy(
                                vc[:, cb, QR * half:QR * half + QR, :],
                                src.rearrange("p (r c) -> p r c", c=COLS)[:, :, KC0[cb]:KC0[cb] + KC])
                    else:
                        if j == 1 and dil:
                            m0 = CK // HALVES * half
                            nc.vector.tensor_copy(kc[:, :, m0:m0 + CK // HALVES],
                                                  src.rearrange("p (m r) -> p r m", r=CL))
                        ins = nc.vector.tensor_copy(kv[:, j - 1, cols], src)
                    ins.then_inc(pj_out, 1)

            def values(p):
                for g in range(NVG):
                    n = min(VB, NV - VB * g)
                    dve.wait_ge(v_tr, NVG * p + g + 1)
                    nc.vector.tensor_copy(vt[:, VB * g:VB * g + n, :],
                                          tr[:, g % 2, 0:P * n].rearrange("p (v f) -> p v f", v=n)
                                          ).then_inc(v_out, 1)

            def tile_bias(m):
                t, i = m // 2, m % 2
                if dil:
                    band = band_start(t) - P * t + P
                    at = A_W * i + band
                    step = BAND_W + (CK - CQ) - CQ * t - band
                    return bias[:, at:at + 2 * step].rearrange("p (a s) -> p a s", s=step)[:, :, 0:BAND]
                cb, rb = t // RBS, t % RBS
                return bias[:, i, rb * 3 + KIND[cb]]

            def step(p, m, first):
                u, b = NU * p + m, m % 2
                if m < NU:
                    dve.wait_ge(qk, u + 1)
                if m == 0 and dil:
                    dve.wait_ge(b_ld, 16 * (p + 1))
                if m == 0 and not dil:
                    dve.wait_ge(b_ready, 2 * RBS * 3 * (p + 1))
                if not (first and m < 2):
                    dve.wait_ge(exped, u - 1)
                if m < 2:
                    nc.vector.memset(sm[:, b, 3:4], 0.0)
                else:
                    nc.vector.reciprocal(sm[:, b, 2:3], sm[:, b, 1:2]).then_inc(rec, 1)
                if m < NU:
                    of, to = sc[:, b, 0:W], t_s[:, b, :]
                    if dil:
                        of, to = (x.rearrange("p (a k) -> p a k", a=2) for x in (of, to))
                    nc.vector.tensor_tensor_reduce(to, of, tile_bias(m), 1.0, 3e38, ALU.add, ALU.min,
                                                   sm[:, b, 0:1]).then_inc(low, 1)
                if m < 2:
                    return
                dve.wait_ge(rec, u - 1)
                if not (first and m < 4):
                    dve.wait_ge(p_tr, u - 3)
                nc.vector.tensor_scalar(pn[:, b, :], ex[:, b, :], sm[:, b, 2:3], None,
                                        ALU.mult).then_inc(divided, 1)

            def output(p, half, first):
                dve.wait_ge(pv, HALVES * p + half + 1)
                if half == 0 and not first:
                    dve.wait_ge(y_st, 16 * p)
                if dil:
                    to = y[:, NB * half:NB * half + NB].rearrange("p (t m r) -> p t r m", r=CL, m=CQ)
                    of = o[:, half, :].rearrange("p (t r m) -> p t r m", r=CL, m=CQ)
                    ins = nc.vector.tensor_copy(to, of)
                else:
                    n = CBS // HALVES
                    to = y[:, :].rearrange("p (b r c w) -> p b r c w", b=RBS, r=QR, c=CBS)
                    of = o[:, half, :].rearrange("p (c b r w) -> p c b r w", c=n, b=RBS, r=QR)
                    for c in range(n):
                        for b in range(RBS):
                            ins = nc.vector.tensor_copy(to[:, b, :, n * half + c], of[:, c, b])
                ins.then_inc(y_out, 1)

            def pair(p, first, last):
                project(p, 1)
                values(p)
                project(p, 0)
                for m in range(NU + 2):
                    step(p, m, first)
                    if m == UN + LAG - 1 and not last:
                        split(p + 1)
                    if m == UN + LAG + 2:
                        output(p, 0, first)
                if not last:
                    project(p + 1, 2)
                output(p, 1, first)

            split(0)
            project(0, 2)
            over_pairs(dve, pair)

        @block.tensor
        def _(pe):
            def project(p, j, half, first=False):
                x = 2 * PROJECTED.index(j) + half
                if x == 0:
                    pe.wait_ge(w_lo, p + 1)
                if not (first and x < 2):
                    pe.wait_ge(pj_out, NPJ * p + x - 1)
                for k in range(KT):
                    for n, (l, r) in enumerate(((wh, ut_hi), (wh, ut_lo), (wl, ut_hi))):
                        last = nc.tensor.matmul(pj[:, half, :], l[:, k, j, :],
                                                r[:, k, NB * half:NB * half + NB],
                                                start=(k == 0 and n == 0), stop=(k == KT - 1 and n == 2))
                last.then_inc(pj_mm, 1)

            def value_source(v):
                if dil:
                    start, step = value_tiles_a()[v]
                    return kv[:, 1, start:start + step * (P - 1) + 1:step]
                rc, cb = v // CBS, v % CBS
                return vc[:, cb, RC * rc:RC * rc + RC, :].rearrange("p r c -> p (r c)")

            def values(p, first):
                pe.wait_ge(pj_out, NPJ * p + 2)
                if not first:
                    pe.wait_ge(p_out, NU * p)
                for g in range(NVG):
                    if g >= 2:
                        pe.wait_ge(v_out, NVG * p + g - 1)
                    for v in range(VB * g, min(VB * g + VB, NV)):
                        at = P * (v - VB * g)
                        last = nc.tensor.transpose(tr[:, g % 2, at:at + P], value_source(v), ident[:, :])
                    last.then_inc(v_tr, 1)

            def score(p, m, first):
                u, b = NU * p + m, m % 2
                t, i = m // 2, m % 2
                if not (first and m < 2):
                    pe.wait_ge(low, u - 1)
                if dil:
                    w0 = band_start(t)
                    nc.tensor.matmul(sc[:, b, 0:BAND], q[:, i, P * t:P * t + P], kv[:, 0, w0:w0 + BAND],
                                     start=True, stop=True, skip_group_check=True)
                    for r in range(CL):
                        last = nc.tensor.matmul(sc[CQ * r:CQ * r + CQ, b, BAND:BAND + CK],
                                                q[:, i, P * t + CQ * r:P * t + CQ * r + CQ], kc[:, r, :],
                                                start=True, stop=True, skip_group_check=True)
                else:
                    cb, rb = t // RBS, t % RBS
                    grid = kv[:, 0, :].rearrange("p (r c) -> p r c", c=COLS)
                    last = nc.tensor.matmul(sc[:, b, 0:W], q[:, i, P * t:P * t + P],
                                            grid[:, 4 * rb:4 * rb + KR, KC0[cb]:KC0[cb] + KC],
                                            start=True, stop=True)
                last.then_inc(qk, 1)

            def turn(p, m, first):
                u, b = NU * p + m, m % 2
                pe.wait_ge(divided, u + 1)
                if m < 2:
                    pe.wait_ge(v_out, NVG * (p + 1))
                else:
                    pe.wait_ge(p_out, u - 1)
                for c in range(NC):
                    last = nc.tensor.transpose(tr[:, b, P * c:P * c + P], pn[:, b, P * c:P * c + P],
                                               ident[:, :])
                last.then_inc(p_tr, 1)

            def multiply(p, half, first):
                pe.wait_ge(p_out, NU * p + UN * (half + 1))
                if not first:
                    pe.wait_ge(y_out, HALVES * (p - 1) + half + 1)
                todo = products(dil, half)
                for n, (v, users, cls) in enumerate(todo):
                    for i in range(2):
                        to = o[HD * i:HD * i + HD, half, :]
                        if cls is not None:
                            to = to.rearrange("p (t r m) -> p t r m", r=CL, m=CQ)[:, :, cls]
                            of = pt[:, i, :, users[0][1], CQ * cls:CQ * cls + CQ]
                        else:
                            t, ch = users[0]
                            to = to[:, P * t:P * (t + len(users))]
                            of = pt[:, i, t, ch]
                            if len(users) == 2:
                                at, step = (t * NC + ch) * P, (NC - 1) * P
                                of = pt_flat[:, i, at:at + 2 * step].rearrange(
                                    "p (a s) -> p a s", s=step)[:, :, 0:P]
                        last = nc.tensor.matmul(to, vt[:, v, HD * i:HD * i + HD], of, start=(n == 0),
                                                stop=(n == len(todo) - 1), skip_group_check=True)
                last.then_inc(pv, 1)

            def pair(p, first, last):
                for half in range(HALVES):
                    project(p, 1, half)
                values(p, first)
                for half in range(HALVES):
                    project(p, 0, half)
                pe.wait_ge(pj_out, NPJ * (p + 1))
                for m in range(NU + LAG):
                    if m < NU:
                        score(p, m, first)
                    if m >= LAG:
                        turn(p, m - LAG, first)
                    if NU - 1 <= m < NU - 1 + HALVES and not last:
                        project(p + 1, 2, m - (NU - 1))
                    if m - LAG == UN - 1:
                        multiply(p, 0, first)
                multiply(p, 1, first)

            for half in range(HALVES):
                project(0, 2, half, True)
            pe.wait_ge(zeroed, 2)
            over_pairs(pe, pair)


def output_projection_phase(nc, top, w_out, y_t, h_t, gate, ut_hi, ut_lo, acc):
    y_ld = [top.sem(f"o_y_ld{b}") for b in range(2)]
    w_ld = [top.sem(f"o_w_ld{b}") for b in range(2)]
    g_ld, h_ld, scaled = top.sem("o_g_ld"), top.sem("o_h_ld"), top.sem("o_scaled")
    y_hi, y_lo, w_hi, w_lo = top.sem("o_y_hi"), top.sem("o_y_lo"), top.sem("o_w_hi"), top.sem("o_w_lo")
    mm, out = top.sem("o_mm"), top.sem("o_out")
    NT = TT * HALVES
    BANKS = 8
    with ExitStack() as st:
        a = Parts(nc, st)
        y = a.sb("o_y", [P, 2, S])
        w = a.sb("o_w", [P, 2, D])
        gates = a.sb("o_gates", [P, D])
        wh = a.sb("o_wh", [P, KT, D], F32R)
        wl = a.sb("o_wl", [P, KT, D], F32R)
        ps = a.ps("o_ps", [P, BANKS, NB])
        block = st.enter_context(nc.Block())

        @block.sync
        def _(sp):
            for k in range(KT):
                b = k % 2
                if k >= 2:
                    sp.wait_ge(y_lo, k - 1)
                    sp.wait_ge(w_lo, k - 1)
                sp.dma_start(w[:, b, :], w_out[P * k:P * k + P, :]).then_inc(w_ld[b], 16)
                if k == 0:
                    sp.dma_start(gates[:, :], gate.broadcast_to([P, D])).then_inc(g_ld, 16)
                sp.dma_start(y[:, b, :], y_t[k]).then_inc(y_ld[b], 16)
            sp.dma_start(acc[:, :, :], h_t.rearrange("(t p) d -> p t d", p=P)).then_inc(h_ld, 16)

        @block.gpsimd
        def _(pool):
            pool.wait_ge(g_ld, 16)
            for k in range(KT):
                pool.wait_ge(w_ld[k % 2], 16 * (k // 2 + 1))
                nc.gpsimd.tensor_tensor(w[:, k % 2, :], w[:, k % 2, :], gates[:, :], ALU.mult).then_inc(scaled, 1)

        @block.scalar
        def _(act):
            for k in range(KT):
                act.wait_ge(y_ld[k % 2], 16 * (k // 2 + 1))
                nc.scalar.copy(ut_hi[:, k, :], y[:, k % 2, :]).then_inc(y_hi, 1)
                act.wait_ge(scaled, k + 1)
                nc.scalar.copy(wh[:, k, :], w[:, k % 2, :]).then_inc(w_hi, 1)

        @block.vector
        def _(dve):
            for k in range(KT):
                dve.wait_ge(y_hi, k + 1)
                nc.vector.tensor_tensor(ut_lo[:, k, :], y[:, k % 2, :], ut_hi[:, k, :].bitcast(F32),
                                        ALU.subtract).then_inc(y_lo, 1)
                dve.wait_ge(w_hi, k + 1)
                nc.vector.tensor_tensor(wl[:, k, :], w[:, k % 2, :], wh[:, k, :].bitcast(F32),
                                        ALU.subtract).then_inc(w_lo, 1)
            dve.wait_ge(h_ld, 16)
            for j in range(NT):
                cols = slice(NB * (j % 2), NB * (j % 2) + NB)
                dve.wait_ge(mm, j + 1)
                nc.vector.tensor_tensor(acc[:, j // 2, cols], ps[:, j % BANKS, :], acc[:, j // 2, cols],
                                        ALU.add).then_inc(out, 1)

        @block.tensor
        def _(pe):
            def block_of(j, k):
                t, half = j // 2, j % 2
                for n, (l, r) in enumerate(((ut_hi, wh), (ut_hi, wl), (ut_lo, wh))):
                    last = nc.tensor.matmul(ps[:, j % BANKS, :], l[:, k, P * t:P * t + P],
                                            r[:, k, NB * half:NB * half + NB],
                                            start=(k == 0 and n == 0), stop=(k == KT - 1 and n == 2))
                if k == KT - 1:
                    last.then_inc(mm, 1)

            for k in range(KT):
                pe.wait_ge(w_lo, k + 1)
                for j in range(BANKS):
                    block_of(j, k)
            for j in range(BANKS, NT):
                pe.wait_ge(out, j - BANKS + 1)
                for k in range(KT):
                    block_of(j, k)


def kernel_program(nc, x, c, w_ada, b_ada, g1, u1, d1, w_in, rpb, w_out, g2, u2, d2, ln_g, ln_b,
                   ident_in, a_bias, b_mask, out):
    mods_row = nc.dram_tensor("mods_row", [1, N_MOD * D], F32, kind="Internal").ap()
    mods = nc.dram_tensor("mods", [1, N_MOD * D], F32, kind="Internal").ap()
    h_t = nc.dram_tensor("scaled_h_before_mix", [S, D], F32, kind="Internal").ap()
    y_t = nc.dram_tensor("mixed_turned", [KT, P, S], F32, kind="Internal").ap()
    tab = nc.dram_tensor("bias_table", [QC, HEADS, TAB_R * TAB_W], F32, kind="Internal").ap()
    ada_v = w_ada.rearrange("l (k p) n -> p (l k) n", p=P)
    with ExitStack() as st:
        top = Parts(nc, st)
        mod_col = top.sb("mod_col", [P, 3 * 2 * KT])
        ident = top.sb("ident", [P, P])
        cs = top.sb("silu_c", [P, KT])
        with nc.cleanup_on_exit():
            modulation_phase(nc, top, c, ada_v, ident_in, rpb, mods_row, ident, cs, tab)
        with nc.cleanup_on_exit():
            columns_phase(nc, top, "c0", 0, 1, mods_row, b_ada, mods, mod_col, ident)
        ut_hi = top.sb("ut_hi", [P, KT, S], F32R)
        ut_lo = top.sb("ut_lo", [P, KT, S], F32R)
        acc = top.sb("acc", [P, TT, D])
        common = (acc, mod_col, ident, ut_hi, ut_lo)

        def gate(j):
            return mods[:, (3 * j + 2) * D:(3 * j + 3) * D]

        def ffn(tag, weights, j, ada, **boundary):
            views = ffn_views(*weights)
            with ExitStack() as inner:
                own = Parts(nc, inner)
                raw = own.sb(tag + "_raw", [P, KT, 2, 2 * P])
                raw_d = own.sb(tag + "_raw_d", [P, 2, D])
                with nc.cleanup_on_exit():
                    boundary_phase(nc, top, tag + "b", *common, enter=j,
                                   prefetch=ffn_prefetch(views, raw, raw_d, top.sem(tag + "_first")), **boundary)
                with nc.cleanup_on_exit():
                    ffn_phase(nc, top, tag, views, raw, raw_d, gate(j), 0.5, ut_hi, ut_lo, acc, ada)

        ffn("f1", (g1, u1, d1), 0, (cs, ada_v, mods_row), x=x)
        with nc.cleanup_on_exit():
            columns_phase(nc, top, "c1", 1, 2, mods_row, b_ada, mods, mod_col, ident)
        with nc.cleanup_on_exit():
            boundary_phase(nc, top, "b1", *common, lng=ln_g[0, 0:1, :], lnb=ln_b[0, 0:1, :], enter=1, store=h_t)
        with nc.cleanup_on_exit():
            attention_phase(nc, top, "a", w_in, 0, 0, ut_hi, ut_lo, acc, ident, a_bias, None, y_t)
        with nc.cleanup_on_exit():
            attention_phase(nc, top, "b", w_in, 3 * D // 2, HP, ut_hi, ut_lo, acc, ident, b_mask, tab, y_t)
        with nc.cleanup_on_exit():
            output_projection_phase(nc, top, w_out, y_t, h_t, gate(1), ut_hi, ut_lo, acc)
        ffn("f2", (g2, u2, d2), 2, None, lng=ln_g[0, 1:2, :], lnb=ln_b[0, 1:2, :])
        with nc.cleanup_on_exit():
            boundary_phase(nc, top, "b3", *common, lng=ln_g[0, 2:3, :], lnb=ln_b[0, 2:3, :], store=out)


def kernel(x, c, w_ada, b_ada, ffn1_w_gate, ffn1_w_up, ffn1_w_down, w_in, rpb, w_out,
           ffn2_w_gate, ffn2_w_up, ffn2_w_down, ln_g, ln_b):
    import concourse.bacc as bacc
    from concourse.bass_utils import run_bass_kernel_spmd

    nc = bacc.Bacc("TRN2", target_bir_lowering=False, num_devices=1)
    arrays = dict(x=x, c=c, w_ada=w_ada, b_ada=b_ada, ffn1_w_gate=ffn1_w_gate, ffn1_w_up=ffn1_w_up,
                  ffn1_w_down=ffn1_w_down, w_in=w_in, rpb=rpb, w_out=w_out, ffn2_w_gate=ffn2_w_gate,
                  ffn2_w_up=ffn2_w_up, ffn2_w_down=ffn2_w_down, ln_g=ln_g, ln_b=ln_b)
    arrays.update(identity=np.eye(P, dtype=np.float32), dilated_bias=dilated_bias(),
                  window_masks=window_masks())
    arrays = {n: np.ascontiguousarray(v) for n, v in arrays.items()}
    d = {n: nc.dram_tensor("in_" + n, list(v.shape), F32, kind="ExternalInput").ap()
         for n, v in arrays.items()}
    out = nc.dram_tensor("out", [1, S, D], F32, kind="ExternalOutput").ap()
    kernel_program(nc, d["x"][0], d["c"], d["w_ada"], d["b_ada"], d["ffn1_w_gate"][0], d["ffn1_w_up"][0],
                   d["ffn1_w_down"][0], d["w_in"][0], d["rpb"], d["w_out"][0], d["ffn2_w_gate"][0],
                   d["ffn2_w_up"][0], d["ffn2_w_down"][0], d["ln_g"], d["ln_b"], d["identity"],
                   d["dilated_bias"], d["window_masks"], out[0])
    got = run_bass_kernel_spmd(nc, [{"in_" + n: v for n, v in arrays.items()}], core_ids=[0])
    return got.results[0]["out"]
```

```python
from contextlib import ExitStack

import concourse.bass as bass
import concourse.mybir as mybir
import numpy as np

F32 = mybir.dt.float32
F32R = mybir.dt.float32r
ALU = mybir.AluOpType
ACT = mybir.ActivationFunctionType
AX = mybir.AxisListType

P = 128
S = 1024
D = 1024
F = 2816
N_MOD = 9
KT = D // P
TT = S // P
NB = 512
HALVES = S // NB
FC = F // P
PAIRS = FC // 2
EARLY = 6
M_LATER = (2 * PAIRS + EARLY) * 256
M_FIRST = N_MOD * D - M_LATER
ALPHA = 2.0 ** 0.25
EPS = 1e-5
HD = 64
HEADS = 8
HP = HEADS // 2
BIG = 1e30

CL = 4
CQ = P // CL
CK = S // CL
BAND = 256
BAND_W = 384
CLS_W = CK + CK - CQ
A_W = BAND_W + CLS_W
A_PAD = 2 * A_W + 256
NAT = (0, 1, TT - 2, TT - 1)
OFFS = tuple(range(HD, S - P - HD + 1, P))
A_VT = len(NAT) + len(OFFS) + 2 * CL

ROWS, COLS = 16, 64
QR, QC = 8, 16
KH, KW = 8, 16
KR, KC = 12, 32
B_K = KR * KC
CBS = COLS // QC
RBS = ROWS // QR
RC = 4
TAB_R, TAB_W = 23, 64
RUN_R = 16
RUN = (RUN_R - 1) * TAB_W + 48
KC0 = tuple(min(max(QC * c - KW // 2, 0), COLS - KC) for c in range(CBS))
KIND = (0, 1, 1, 2)


def slopes():
    return 2.0 ** (-8.0 * np.arange(1, HEADS + 1) / HEADS)


def dilated_bias():
    q = np.arange(P)
    tok = 4 * (q % CQ) + q // CQ
    rel_band = np.arange(BAND_W)[None, :] - P - tok[:, None]
    rel_cls = np.arange(CLS_W)[None, :] - (CK - CQ) - (q % CQ)[:, None]
    count = (np.abs(rel_cls) <= 64).astype(np.float64) + (rel_cls % 4 == 0)
    out = np.zeros((P, HP, A_PAD), np.float32)
    for h, s in enumerate(slopes()):
        band = np.where(np.abs(rel_band) <= 64, s * np.abs(rel_band), BIG)
        cls = np.where(count > 0, s * 4 * np.abs(rel_cls) - np.log(np.maximum(count, 1)), BIG)
        at = (h % 2) * A_W
        out[:, h // 2, at:at + A_W] = np.concatenate([band, cls], axis=1)
    return out


def window_masks():
    out = np.zeros((P, RBS * 3, KR, KC), np.float32)
    for rb in range(RBS):
        for cb in range(CBS):
            for q in range(P):
                r, c = QR * rb + q // QC, QC * cb + q % QC
                r0 = min(max(r - KH // 2, 0), ROWS - KH)
                c0 = min(max(c - KW // 2, 0), COLS - KW)
                rows = 4 * rb + np.arange(KR)
                cols = KC0[cb] + np.arange(KC)
                ok = ((rows >= r0) & (rows < r0 + KH))[:, None] & ((cols >= c0) & (cols < c0 + KW))
                out[q, rb * 3 + KIND[cb]] = np.where(ok, 0.0, BIG)
    return out.reshape(P, RBS * 3, B_K)


class Parts:

    def __init__(self, nc, stack):
        self.nc, self.stack = nc, stack

    def sb(self, name, shape, dt=F32):
        return self.stack.enter_context(self.nc.sbuf_tensor(name, shape, dt))

    def ps(self, name, shape, dt=F32):
        return self.stack.enter_context(self.nc.psum_tensor(name, shape, dt))

    def sem(self, name):
        return self.nc.alloc_semaphore(name=name)


def modulation_phase(nc, top, c, w_ada, b_ada, ident_in, rpb, mods, ident, cs, tab, mod_col, x, acc, nrm):
    n = 4
    cw = M_FIRST // n
    tw = cw // 4
    rows = M_FIRST // P
    in_ld, w_ld = top.sem("m_in_ld"), [top.sem(f"m_w_ld{b}") for b in range(n)]
    x_ld = [top.sem(f"m_x_ld{t}") for t in range(TT)]
    b_ld, grid_ld, summed = top.sem("m_b_ld"), top.sem("m_grid_ld"), top.sem("m_summed")
    turned_s, columns = top.sem("m_turned"), top.sem("m_columns")
    c_ready, mm_done, row_done = top.sem("m_c_ready"), top.sem("m_mm"), top.sem("m_row")
    row_st, rpb_ld, tab_st = top.sem("m_row_st"), top.sem("m_rpb_ld"), top.sem("m_tab_st")
    zeroed, neg = top.sem("m_zeroed"), top.sem("m_neg")
    nr, nw = rpb.shape[2:]
    with ExitStack() as st:
        a = Parts(nc, st)
        w = a.sb("m_w", [P, 2, KT, cw])
        grid = a.sb("m_grid", [rows, P])
        bgrid = a.sb("m_bgrid", [rows, P])
        ln = Normaliser(nc, top, a, "m_ln")
        ccol = a.sb("m_c", [P, KT])
        row = a.sb("m_rowbuf", [1, M_FIRST])
        raw = a.sb("m_raw", [HEADS, nr, nw])
        pad = a.sb("m_pad", [HEADS, TAB_R, TAB_W])
        sums = a.ps("m_sums", [P, 2, NB])
        turned = a.ps("m_turned_ps", [P, NB])
        block = st.enter_context(nc.Block())

        @block.sync
        def _(sp):
            with nc.allow_non_contiguous_dma(reason="one short vector"):
                sp.dma_start(ccol[:, :], c.rearrange("o (k p) -> p (o k)", p=P)).then_inc(in_ld, 16)
            def load_w(i):
                if i >= 2:
                    sp.wait_ge(mm_done, i - 1)
                sp.dma_start(w[:, i % 2], w_ada[:, :, cw * i:cw * i + cw]).then_inc(w_ld[i], 16)

            def load_x(t):
                sp.dma_start(acc[:, t, :], x[P * t:P * t + P, :]).then_inc(x_ld[t], 16)

            load_w(0)
            load_w(1)
            for t in range(TT // 2):
                load_x(t)
            load_w(2)
            load_w(3)
            for t in range(TT // 2, TT):
                load_x(t)
            sp.dma_start(bgrid[:, :], b_ada[:, 0:M_FIRST].rearrange("o (r p) -> (o r) p", p=P)).then_inc(b_ld, 16)
            sp.wait_ge(row_done, 4 * n)
            sp.dma_start(mods[:, 0:M_FIRST], row[:, :]).then_inc(row_st, 16)
            sp.wait_ge(row_st, 16)
            sp.dma_start(grid[:, :], mods[:, 0:M_FIRST].rearrange("o (r p) -> (o r) p", p=P)).then_inc(grid_ld, 16)

        @block.scalar
        def _(act):
            act.dma_start(ident[:, :], ident_in).then_inc(in_ld, 16)
            act.dma_start(raw[:, :, :], rpb[0]).then_inc(rpb_ld, 16)
            act.wait_ge(in_ld, 32)
            nc.scalar.activation(cs[:, :], ccol[:, :], ACT.Silu).then_inc(c_ready, 1)
            act.wait_ge(neg, 1)
            flat = pad[:, :, :].rearrange("h r w -> h (r w)")
            for m in range(QC):
                shift = QC - 1 - m
                act.dma_start(tab[m, :, 0:TAB_R * TAB_W - shift],
                              flat[:, shift:TAB_R * TAB_W]).then_inc(tab_st, 16)
            for g in range(TT // 2):
                ln.root(act, g)
                for t in (2 * g, 2 * g + 1):
                    ln.normalise(act, nrm[:, t, :], acc[:, t, :], t)
            act.wait_ge(tab_st, 16 * QC)

        @block.tensor
        def _(pe):
            pe.wait_ge(c_ready, 1)
            for i in range(n):
                pe.wait_ge(w_ld[i], 16)
                if i >= 2:
                    pe.wait_ge(row_done, 4 * (i - 1))
                for k in range(KT):
                    for j in range(4):
                        last = nc.tensor.matmul(sums[32 * j:32 * j + 1, i % 2, 0:tw], cs[:, k:k + 1],
                                                w[:, i % 2, k, tw * j:tw * j + tw],
                                                start=(k == 0), stop=(k == KT - 1))
                last.then_inc(mm_done, 1)
            pe.wait_ge(summed, 1)
            nc.tensor.transpose(turned[:, 0:rows], grid[:, :], ident[0:rows, 0:rows]).then_inc(turned_s, 1)

        @block.vector
        def _(dve):
            nc.vector.memset(pad[:, :, :], 0.0).then_inc(zeroed, 1)
            dve.wait_ge(zeroed, 1)
            dve.wait_ge(rpb_ld, 16)
            r0, c0 = (TAB_R - nr) // 2, (TAB_W - 1 - nw) // 2
            nc.vector.tensor_scalar(pad[:, r0:r0 + nr, c0:c0 + nw], raw[:, :, :], -1.0, None,
                                    ALU.mult).then_inc(neg, 1)
            def normalise(g):
                for t in (2 * g, 2 * g + 1):
                    dve.wait_ge(x_ld[t], 16)
                    ln.statistics(dve, acc[:, t, :], t)
                ln.coefficients(dve, g)

            for i in range(n):
                dve.wait_ge(mm_done, i + 1)
                for j in range(4):
                    at = cw * i + tw * j
                    nc.vector.tensor_copy(row[0:1, at:at + tw],
                                          sums[32 * j:32 * j + 1, i % 2, 0:tw]).then_inc(row_done, 1)
                if i == 1:
                    normalise(0)
                    normalise(1)
            normalise(2)
            normalise(3)
            dve.wait_ge(b_ld, 16)
            dve.wait_ge(grid_ld, 16)
            nc.vector.tensor_tensor(grid[:, :], grid[:, :], bgrid[:, :], ALU.add).then_inc(summed, 1)
            dve.wait_ge(turned_s, 1)
            nc.vector.tensor_copy(mod_col[:, 0:KT], turned[:, 0:KT]).then_inc(columns, 1)
            nc.vector.tensor_scalar(mod_col[:, KT:rows], turned[:, KT:rows], 1.0, None, ALU.add).then_inc(columns, 1)


class Normaliser:

    def __init__(self, nc, top, a, tag):
        self.nc = nc
        self.sm = a.sb(tag + "_sm", [P, TT, 20])
        self.eps = a.sb(tag + "_eps", [P, 1])
        self.small, self.eps_set = top.sem(tag + "_small"), top.sem(tag + "_eps_set")
        self.var_done, self.std_done, self.coef_done = (top.sem(f"{tag}_{n}") for n in ("var", "std", "coef"))
        self.normed = top.sem(tag + "_normed")
        self.count = 0

    def chained(self, dve, ins):
        self.count += 1
        ins.then_inc(self.small, 1)
        dve.wait_ge(self.small, self.count)

    def statistics(self, dve, of, t):
        nc, s_ = self.nc, self.sm[:, t, :]
        if t == 0:
            nc.vector.memset(self.eps[:, :], EPS).then_inc(self.eps_set, 1)
        nc.vector.bn_stats(s_[:, 0:6], of[:, 0:NB])
        self.chained(dve, nc.vector.bn_stats(s_[:, 6:12], of[:, NB:D]))
        nc.vector.bn_aggr(s_[:, 12:14], s_[:, 0:12]).then_inc(self.var_done, 1)

    def root(self, act, g):
        nc = self.nc
        act.wait_ge(self.var_done, 2 * g + 2)
        if g == 0:
            act.wait_ge(self.eps_set, 1)
        for t in (2 * g, 2 * g + 1):
            nc.scalar.activation(self.sm[:, t, 14:15], self.sm[:, t, 13:14], ACT.Sqrt,
                                 bias=self.eps[:, 0:1]).then_inc(self.std_done, 1)

    def coefficients(self, dve, g):
        nc = self.nc
        mean, var, std, y_, a_, b_, r, nb = (self.sm[:, 2 * g:2 * g + 2, i] for i in range(12, 20))
        dve.wait_ge(self.std_done, 2 * g + 2)
        self.chained(dve, nc.vector.reciprocal(y_, std))
        self.chained(dve, nc.vector.scalar_tensor_tensor(a_, var, EPS, y_, ALU.add, ALU.mult))
        self.chained(dve, nc.vector.scalar_tensor_tensor(b_, a_, -0.5, y_, ALU.mult, ALU.mult))
        self.chained(dve, nc.vector.scalar_tensor_tensor(r, b_, 1.5, y_, ALU.add, ALU.mult))
        nc.vector.scalar_tensor_tensor(nb, mean, -1.0, r, ALU.mult, ALU.mult).then_inc(self.coef_done, 1)

    def normalise(self, act, to, of, t):
        act.wait_ge(self.coef_done, t // 2 + 1)
        self.nc.scalar.activation(to, of, ACT.Identity, bias=self.sm[:, t, 19:20],
                                  scale=self.sm[:, t, 18:19]).then_inc(self.normed, 1)


class Leaving:
    ON_POOL = 2

    def __init__(self, nc, top, a, tag, acc, rows, lng, lnb, out=None):
        self.nc, self.acc, self.rows, self.lng, self.lnb, self.out = nc, acc, rows, lng, lnb, out
        self.ln = Normaliser(nc, top, a, tag + "_leave")
        self.bc_ld, self.gained, self.stored = (top.sem(f"{tag}_leave_{n}") for n in ("bc_ld", "gained", "stored"))
        self.gained_v = top.sem(tag + "_leave_gained_v")
        self.shifted_p, self.shifted_v = top.sem(tag + "_leave_shifted_p"), top.sem(tag + "_leave_shifted_v")

    def load(self, sp):
        for i, r in enumerate((self.lng, self.lnb)):
            sp.dma_start(self.rows[:, i, :], r.broadcast_to([P, D])).then_inc(self.bc_ld, 16)

    def store(self, sp):
        if self.out is None:
            return
        for t in range(TT):
            if t < self.ON_POOL:
                sp.wait_ge(self.shifted_p, t + 1)
            else:
                sp.wait_ge(self.shifted_v, (t + 1 if t < TT - 2 else TT) - self.ON_POOL)
            sp.dma_start(self.out[P * t:P * t + P, :], self.acc[:, t, :]).then_inc(self.stored, 16)
        sp.wait_ge(self.stored, 16 * TT)

    def affine(self, pool):
        nc, acc, rows = self.nc, self.acc, self.rows
        pool.wait_ge(self.bc_ld, 32)
        for t in range(TT - 1):
            pool.wait_ge(self.ln.normed, t + 1)
            nc.gpsimd.tensor_tensor(acc[:, t, :], acc[:, t, :], rows[:, 0, :], ALU.mult).then_inc(self.gained, 1)
            if t < self.ON_POOL:
                pool.wait_ge(self.gained, t + 1)
                nc.gpsimd.tensor_tensor(acc[:, t, :], acc[:, t, :], rows[:, 1, :], ALU.add).then_inc(self.shifted_p, 1)

    def normalise(self, act):
        for g in range(TT // 2):
            self.ln.root(act, g)
            for t in (2 * g, 2 * g + 1):
                self.ln.normalise(act, self.acc[:, t, :], self.acc[:, t, :], t)

    def summed(self, dve, t):
        self.ln.statistics(dve, self.acc[:, t, :], t)
        if t % 2 == 0 and t > 0:
            self.ln.coefficients(dve, t // 2 - 1)

    def shifts(self, dve, tiles):
        dve.wait_ge(self.bc_ld, 32)
        for t in tiles:
            self.shift(dve, t)

    def finish(self, dve, first=ON_POOL):
        self.ln.coefficients(dve, TT // 2 - 1)
        self.shifts(dve, [*range(first, TT - 2), TT - 1, TT - 2])

    def shift(self, dve, t):
        nc, acc = self.nc, self.acc
        if t < TT - 1:
            dve.wait_ge(self.gained, t + 1)
        else:
            dve.wait_ge(self.ln.normed, TT)
            nc.vector.tensor_tensor(acc[:, t, :], acc[:, t, :], self.rows[:, 0, :], ALU.mult).then_inc(self.gained_v, 1)
            dve.wait_ge(self.gained_v, 1)
        nc.vector.tensor_tensor(acc[:, t, :], acc[:, t, :], self.rows[:, 1, :], ALU.add).then_inc(self.shifted_v, 1)


def boundary_phase(nc, top, tag, acc, mod_col, ident, ut_hi, ut_lo, enter, nrm=None, store=None, prefetch=None,
                   loaded=(), split_first=None, begin=None, mods=None):
    def sem(name):
        return top.sem(f"{tag}_{name}")

    stored, scaled = sem("stored"), sem("scaled")
    ready = nrm is not None
    tr_done, hi_done, lo_done = sem("tr"), sem("hi"), sem("lo")
    mod_done = [sem("mod_v"), sem("mod_s")]
    w_hi, w_lo = sem("w_hi"), sem("w_lo")
    m_ld, m_turned, m_col = sem("m_ld"), sem("m_turned"), sem("m_col")
    n_mods = (3 - enter) * 3 * KT
    G = TT // HALVES
    MB = 4
    with ExitStack() as st:
        a = Parts(nc, st)
        ln = Normaliser(nc, top, a, tag)
        if not ready:
            nrm = a.sb(tag + "_nrm", [P, TT, D])
        mod = a.sb(tag + "_mod", [P, MB, NB])
        turned = a.ps(tag + "_turned", [P, MB, NB])
        if mods is not None:
            grid = a.sb(tag + "_grid", [n_mods, P])
            m_ps = a.ps(tag + "_mods", [P, NB])
        block = st.enter_context(nc.Block())

        def modulate(y, eng):
            eng.wait_ge(tr_done, y + 1)
            if y >= MB:
                eng.wait_ge(lo_done, y - MB + 1)
            m = 16 * enter + y % KT
            shift, scale = mod_col[:, m:m + 1], mod_col[:, m + 8:m + 9]
            if y % 2 == 0:
                nc.vector.tensor_scalar(mod[:, y % MB, :], turned[:, y % MB, :], scale, shift, ALU.mult,
                                        ALU.add).then_inc(mod_done[0], 1)
            else:
                nc.scalar.activation(mod[:, y % MB, :], turned[:, y % MB, :], ACT.Identity, bias=shift,
                                     scale=scale).then_inc(mod_done[1], 1)

        @block.sync
        def _(sp):
            if mods is not None:
                sp.dma_start(grid[:, :], mods[:, 3 * enter * D:].rearrange("o (r p) -> (o r) p", p=P)
                             ).then_inc(m_ld, 16)
            if prefetch is not None:
                prefetch(sp)
            if store is not None:
                for t in range(TT):
                    sp.wait_ge(scaled, t + 1)
                    sp.dma_start(store[P * t:P * t + P, :], acc[:, t, :]).then_inc(stored, 16)
                sp.wait_ge(stored, 16 * TT)
            for s_, n in loaded:
                sp.wait_ge(s_, n)

        @block.gpsimd
        def _(pool):
            for t in range(TT):
                if not ready:
                    pool.wait_ge(ln.normed, t + 1)
                nc.gpsimd.tensor_scalar(acc[:, t, :], acc[:, t, :], ALPHA, 1.0, ALU.mult,
                                        ALU.mult).then_inc(scaled, 1)
                if split_first is not None and t == TT // 2 - 1:
                    raw, hi, lo = split_first
                    pool.wait_ge(w_hi, 1)
                    nc.gpsimd.tensor_tensor(lo, raw, hi.bitcast(F32), ALU.subtract).then_inc(w_lo, 1)

        @block.scalar
        def _(act):
            def high(y):
                if y % 2:
                    modulate(y, act)
                act.wait_ge(mod_done[y % 2], y // 2 + 1)
                nc.scalar.copy(ut_hi[:, y % KT, NB * (y // KT):NB * (y // KT) + NB],
                               mod[:, y % MB, :]).then_inc(hi_done, 1)

            for g in range(TT // 2):
                if not ready:
                    ln.root(act, g)
                if 2 * g == G and mods is not None:
                    act.wait_ge(m_col, 2 * (3 - enter))
                if 2 * g >= G:
                    for y in range(4 * g - KT, 4 * g - KT + 4):
                        high(y)
                for t in (2 * g, 2 * g + 1) if not ready else ():
                    ln.normalise(act, nrm[:, t, :], acc[:, t, :], t)
                if split_first is not None and g == 1:
                    for s_, n in loaded:
                        act.wait_ge(s_, n)
                    nc.scalar.copy(split_first[1], split_first[0]).then_inc(w_hi, 1)
            for y in range(KT, 2 * KT):
                high(y)

        @block.tensor
        def _(pe):
            if mods is not None:
                pe.wait_ge(m_ld, 16)
                nc.tensor.transpose(m_ps[:, 0:n_mods], grid[:, :], ident[0:n_mods, 0:n_mods]).then_inc(m_turned, 1)
            for y in range(2 * KT):
                if begin is not None and y >= KT:
                    if y == KT:
                        pe.wait_ge(lo_done, KT)
                        pe.wait_ge(w_lo, 1)
                        begin(0)
                        begin(1)
                    if y < 2 * KT - 2:
                        begin(y - KT + 2)
                if not ready:
                    pe.wait_ge(ln.normed, G * (y // KT + 1))
                if y >= MB:
                    pe.wait_ge(mod_done[y % 2], (y - MB) // 2 + 1)
                for g in range(G):
                    last = nc.tensor.transpose(turned[:, y % MB, P * g:P * g + P],
                                               nrm[:, G * (y // KT) + g, P * (y % KT):P * (y % KT) + P],
                                               ident[:, :])
                last.then_inc(tr_done, 1)

        @block.vector
        def _(dve):
            def low(y):
                dve.wait_ge(hi_done, y + 1)
                cols = slice(NB * (y // KT), NB * (y // KT) + NB)
                nc.vector.tensor_tensor(ut_lo[:, y % KT, cols], mod[:, y % MB, :],
                                        ut_hi[:, y % KT, cols].bitcast(F32), ALU.subtract).then_inc(lo_done, 1)

            def blocks(ys):
                for y in ys:
                    if y % 2 == 0:
                        modulate(y, dve)
                    if y - ys[0] >= 2:
                        low(y - 2)
                for y in ys[-2:]:
                    low(y)

            for g in range(TT // 2):
                for t in (2 * g, 2 * g + 1) if not ready else ():
                    ln.statistics(dve, acc[:, t, :], t)
                if 2 * g >= G:
                    blocks(range(4 * g - KT, 4 * g - KT + 4))
                if not ready:
                    ln.coefficients(dve, g)
                if g == 1 and mods is not None:
                    dve.wait_ge(m_turned, 1)
                    src = m_ps[:, 0:n_mods].rearrange("p (j w k) -> p j w k", j=3 - enter, w=3)
                    dst = mod_col[:, :].rearrange("p (j w k) -> p j w k", j=3, w=2)
                    for j in range(3 - enter):
                        nc.vector.tensor_copy(dst[:, enter + j, 0], src[:, j, 0]).then_inc(m_col, 1)
                        nc.vector.tensor_scalar(dst[:, enter + j, 1], src[:, j, 1], 1.0, None, ALU.add
                                                ).then_inc(m_col, 1)
                    dve.wait_ge(m_col, 2 * (3 - enter))
            blocks(range(KT, 2 * KT))


def ffn_views(w_gate, w_up, w_down):
    return (w_gate.rearrange("(k p) n -> p k n", p=P), w_up.rearrange("(k p) n -> p k n", p=P),
            w_down.rearrange("(f p) n -> p f n", p=P))


def ffn_prefetch(views, raw, raw_d, loaded):
    def prefetch(sp):
        gate_v, up_v, down_v = views
        sp.dma_start(raw[:, :, 0, :], gate_v[:, :, 0:2 * P]).then_inc(loaded, 16)
        sp.dma_start(raw[:, :, 1, :], up_v[:, :, 0:2 * P]).then_inc(loaded, 16)
        sp.dma_start(raw_d[:, :, :], down_v[:, 0:2, :]).then_inc(loaded, 16)
    return prefetch


def ffn_weights(a, tag):
    return a.sb(tag + "_wh", [P, 2, KT, 2, P], F32R), a.sb(tag + "_wl", [P, 2, KT, 2, P], F32R)


def ffn_phase(nc, top, tag, views, raw, raw_d, gate, resid, ut_hi, ut_lo, acc, ada, lng, lnb, out, gu,
              begun=None):
    ld_gu, ld_d = top.sem(tag + "_ld_gu"), top.sem(tag + "_ld_d")
    w_hi, w_lo = [top.sem(f"{tag}_w_hi{i}") for i in range(2)], [top.sem(f"{tag}_w_lo{i}") for i in range(2)]
    d_hi, d_lo = top.sem(tag + "_d_hi"), top.sem(tag + "_d_lo")
    gu_mm, silu_done, mul_done = top.sem(tag + "_gu_mm"), top.sem(tag + "_silu"), top.sem(tag + "_mul")
    hid_hi_s, hid_lo_s = top.sem(tag + "_hid_hi"), top.sem(tag + "_hid_lo")
    d_mm, d_add = top.sem(tag + "_d_mm"), top.sem(tag + "_d_add")
    g_ld, g_half, scaled = top.sem(tag + "_g_ld"), top.sem(tag + "_g_half"), top.sem(tag + "_scaled")
    NT = TT * HALVES
    DB = 4 if ada is None else 3
    AW = 256
    if ada is not None:
        cs, w_ada, b_ada, mods = ada
        b_ld = top.sem(tag + "_b_ld")
        a_ld, a_mm, a_part = top.sem(tag + "_a_ld"), top.sem(tag + "_a_mm"), top.sem(tag + "_a_part")
        a_row, a_st = top.sem(tag + "_a_row"), top.sem(tag + "_a_st")
    gate_v, up_v, down_v = views
    with ExitStack() as st:
        a = Parts(nc, st)
        gates = a.sb(tag + "_gates", [P, D])
        if begun is not None:
            wh, wl = begun
        else:
            wh, wl = ffn_weights(a, tag)
        dh = a.sb(tag + "_dh", [P, 2, D], F32R)
        dl = a.sb(tag + "_dl", [P, 2, D], F32R)
        hid_hi = a.sb(tag + "_hidh", [P, 2, S], F32R)
        hid_lo = a.sb(tag + "_hidl", [P, 2, S], F32R)
        sil = a.sb(tag + "_sil", [P, 2, NB])
        prod = a.sb(tag + "_prod", [P, 2, NB])
        dp = a.ps(tag + "_dp", [P, DB, NB])
        if ada is not None:
            aw = a.sb(tag + "_aw", [P, KT, AW])
            arow = a.sb(tag + "_arow", [33, 2, AW])
            am = a.ps(tag + "_am", [P, 2, AW])
            rows = aw[:, :, :].rearrange("p (i k) n -> p i (k n)", i=2)
        else:
            rows = a.sb(tag + "_rows", [P, 2, D])
        leaving = Leaving(nc, top, a, tag, acc, rows, lng, lnb, out)
        block = st.enter_context(nc.Block())

        @block.sync
        def _(sp):
            def load_gu(q):
                sp.wait_ge(w_lo[1], q)
                cols = bass.ds(q * 2 * P, 2 * P)
                sp.dma_start(raw[:, :, 0, :], gate_v[:, :, cols]).then_inc(ld_gu, 16)
                sp.dma_start(raw[:, :, 1, :], up_v[:, :, cols]).then_inc(ld_gu, 16)

            def load_d(q):
                sp.wait_ge(d_lo, q)
                sp.dma_start(raw_d[:, :, :], down_v[:, bass.ds(q * 2, 2), :]).then_inc(ld_d, 16)

            def load_b(r):
                if ada is not None:
                    sp.dma_start(arow[32:33, :, :].rearrange("p c n -> p (c n)"),
                                 b_ada[:, bass.ds(r * 2 * AW + M_FIRST, 2 * AW)]).then_inc(b_ld, 16)

            def store_row(r):
                if ada is not None:
                    sp.wait_ge(a_row, 2 * r + 2)
                    sp.dma_start(mods[:, bass.ds(r * 2 * AW + M_FIRST, 2 * AW)],
                                 arow[0:1, :, :].rearrange("p c n -> p (c n)")).then_inc(a_st, 16)

            load_b(0)
            if ada is None:
                sp.dma_start(gates[:, :], gate.broadcast_to([P, D])).then_inc(g_ld, 16)
            load_gu(1)
            for r in range(EARLY // 2 if ada is not None else 0):
                store_row(r)
                load_b(r + 1)
                if (r + 1) * 2 * AW == D:
                    sp.wait_ge(a_st, 16 * (r + 1))
                    sp.dma_start(gates[:, :], gate.broadcast_to([P, D])).then_inc(g_ld, 16)
            store_row(EARLY // 2)
            load_b(EARLY // 2 + 1)
            load_d(1)
            with sp.Fori(2, PAIRS) as q:
                load_gu(q)
                load_d(q)
                store_row(q + (EARLY // 2 - 1))
                load_b(q + EARLY // 2)
            store_row(PAIRS + EARLY // 2 - 1)
            if ada is not None:
                sp.wait_ge(a_st, 16 * (PAIRS + EARLY // 2))
                sp.wait_ge(a_mm, 2 * PAIRS + EARLY)
            leaving.load(sp)
            leaving.store(sp)

        @block.gpsimd
        def _(pool):
            def scale(q, first):
                if not first:
                    pool.wait_ge(ld_d, 16 * q)
                for i in range(2):
                    ins = nc.gpsimd.tensor_tensor(raw_d[:, i, :], raw_d[:, i, :], gates[:, :], ALU.mult)
                ins.then_inc(scaled, 1)

            def load_ada(c, first=False):
                if ada is not None:
                    if not first:
                        pool.wait_ge(a_mm, c)
                    pool.dma_start(aw[:, :, :], w_ada[:, :, bass.ds(c * AW + M_FIRST, AW)]).then_inc(a_ld, 16)

            pool.sem_inc(d_add, NT)
            for c in range(EARLY + 1):
                load_ada(c, c == 0)
            pool.wait_ge(g_ld, 16)
            nc.gpsimd.tensor_scalar(gates[:, :], gates[:, :], resid, 1.0, ALU.mult, ALU.mult).then_inc(g_half, 1)
            pool.wait_ge(g_half, 1)
            scale(0, True)
            load_ada(EARLY + 1)
            with pool.Fori(1, PAIRS) as q:
                load_ada(q * 2 + EARLY)
                scale(q, False)
                load_ada(q * 2 + (EARLY + 1))
            leaving.affine(pool)

        @block.scalar
        def _(act):
            def split_gu(q, i, first):
                if not first:
                    act.wait_ge(ld_gu, 32 * q)
                    act.wait_ge(gu_mm, 4 * q + 2 * i - 2)
                nc.scalar.copy(wh[:, i], raw[:, :, :, P * i:P * i + P]).then_inc(w_hi[i], 1)

            def split_d(q, first):
                act.wait_ge(scaled, q + 1)
                if not first:
                    act.wait_ge(d_mm, NT * q)
                nc.scalar.copy(dh[:, :, :], raw_d[:, :, :]).then_inc(d_hi, 1)

            def silu(q, i, first):
                for half in range(2):
                    s_ = 4 * q + 2 * i + half
                    act.wait_ge(gu_mm, s_ + 1)
                    if not first:
                        act.wait_ge(mul_done, s_ - 1)
                    nc.scalar.activation(sil[:, half, :], gu[:, half, 0, :],
                                         ACT.Silu).then_inc(silu_done, 1)

            def split_hid(q, i, first):
                for half in range(2):
                    s_ = 4 * q + 2 * i + half
                    act.wait_ge(mul_done, s_ + 1)
                    if not first:
                        act.wait_ge(d_mm, NT * q)
                    nc.scalar.copy(hid_hi[:, i, NB * half:NB * half + NB],
                                   prod[:, half, :]).then_inc(hid_hi_s, 1)

            def body(q, ahead):
                silu(q, 0, False)
                if ahead:
                    split_gu(q + 1, 0, False)
                split_hid(q, 0, False)
                split_d(q, False)
                silu(q, 1, False)
                split_hid(q, 1, False)
                if ahead:
                    split_gu(q + 1, 1, False)

            if begun is not None:
                act.sem_inc(w_hi[0], 1)
            for i in range(2) if begun is None else [1]:
                split_gu(0, i, True)
            silu(0, 0, True)
            split_gu(1, 0, False)
            split_hid(0, 0, True)
            silu(0, 1, False)
            split_hid(0, 1, True)
            split_gu(1, 1, False)
            split_d(0, True)
            with act.Fori(1, PAIRS - 1) as q:
                body(q, True)
            body(PAIRS - 1, False)
            leaving.normalise(act)

        @block.vector
        def _(dve):
            def split_gu(q, i):
                dve.wait_ge(w_hi[i], q + 1)
                nc.vector.tensor_tensor(wl[:, i], raw[:, :, :, P * i:P * i + P], wh[:, i].bitcast(F32),
                                        ALU.subtract).then_inc(w_lo[i], 1)

            def split_d(q):
                dve.wait_ge(d_hi, q + 1)
                nc.vector.tensor_tensor(dl[:, :, :], raw_d[:, :, :], dh[:, :, :].bitcast(F32),
                                        ALU.subtract).then_inc(d_lo, 1)

            def mul(q, i, first, halves=(0, 1)):
                for half in halves:
                    s_ = 4 * q + 2 * i + half
                    dve.wait_ge(silu_done, s_ + 1)
                    if not first:
                        dve.wait_ge(hid_lo_s, s_ - 1)
                    nc.vector.tensor_tensor(prod[:, half, :], sil[:, half, :], gu[:, half, 1, :],
                                            ALU.mult).then_inc(mul_done, 1)

            def split_hid(q, i):
                for half in range(2):
                    s_ = 4 * q + 2 * i + half
                    cols = slice(NB * half, NB * half + NB)
                    dve.wait_ge(hid_hi_s, s_ + 1)
                    nc.vector.tensor_tensor(hid_lo[:, i, cols], prod[:, half, :],
                                            hid_hi[:, i, cols].bitcast(F32),
                                            ALU.subtract).then_inc(hid_lo_s, 1)

            def add_down(q, tiles=range(TT)):
                for j in range(2 * tiles[0], 2 * tiles[-1] + 2):
                    t, half = j // 2, j % 2
                    cols = slice(NB * half, NB * half + NB)
                    dve.wait_ge(d_mm, NT * q + j + 1)
                    dve.wait_ge(d_add, NT * q + j + 1)
                    nc.vector.tensor_tensor(acc[:, t, cols], dp[:, j % DB, :], acc[:, t, cols],
                                            ALU.add).then_inc(d_add, 1)

            def modulation(r, i, first=False):
                if ada is None:
                    return
                dve.wait_ge(a_mm, 2 * r + i + 1)
                dve.wait_ge(b_ld, 16 * (r + 1))
                if not first:
                    dve.wait_ge(a_st, 16 * r)
                nc.vector.tensor_tensor(arow[0:1, i, :], am[0:1, i, :], arow[32:33, i, :], ALU.add).then_inc(a_part, 1)
                for j in range(1, 4):
                    dve.wait_ge(a_part, 6 * r + 3 * i + j)
                    nc.vector.tensor_tensor(arow[0:1, i, :], am[32 * j:32 * j + 1, i, :], arow[0:1, i, :],
                                            ALU.add).then_inc(a_part if j < 3 else a_row, 1)

            def body(q, ahead):
                mul(q, 0, False)
                add_down(q - 1)
                split_hid(q, 0)
                modulation(q + EARLY // 2, 0)
                split_d(q)
                if ahead:
                    split_gu(q + 1, 0)
                mul(q, 1, False)
                split_hid(q, 1)
                if ahead:
                    split_gu(q + 1, 1)
                modulation(q + EARLY // 2, 1)

            if begun is not None:
                dve.sem_inc(w_lo[0], 1)
            for i in range(2) if begun is None else [1]:
                split_gu(0, i)
            modulation(0, 0, True)
            mul(0, 0, True, [0])
            modulation(0, 1, True)
            modulation(1, 0)
            mul(0, 0, True, [1])
            modulation(1, 1)
            split_gu(1, 0)
            split_hid(0, 0)
            modulation(2, 0)
            mul(0, 1, False, [0])
            modulation(2, 1)
            modulation(3, 0)
            mul(0, 1, False, [1])
            modulation(3, 1)
            split_hid(0, 1)
            split_gu(1, 1)
            split_d(0)
            with dve.Fori(1, PAIRS - 1) as q:
                body(q, True)
            body(PAIRS - 1, False)
            for t in range(TT):
                add_down(PAIRS - 1, [t])
                dve.wait_ge(d_add, NT * PAIRS + 2 * t + 2)
                leaving.summed(dve, t)
            leaving.finish(dve)

        @block.tensor
        def _(pe):
            def gate_up(q, i, first, between=None, halves=(0, 1)):
                pe.wait_ge(w_lo[i], q + 1)
                for half in halves:
                    s_ = 4 * q + 2 * i + half
                    cols = slice(NB * half, NB * half + NB)
                    if not first:
                        pe.wait_ge(mul_done, s_ - 1)
                    for g in range(2):
                        for k in range(KT):
                            for n, (l, r) in enumerate(((wh, ut_hi), (wh, ut_lo), (wl, ut_hi))):
                                last = nc.tensor.matmul(gu[:, half, g, :], l[:, i, k, g, :],
                                                        r[:, k, cols], start=(k == 0 and n == 0),
                                                        stop=(k == KT - 1 and n == 2))
                        if g == 1:
                            last.then_inc(gu_mm, 1)
                        if between is not None:
                            between(2 * half + g)

            def down(q, first=False):
                pe.wait_ge(hid_lo_s, 4 * (q + 1))
                pe.wait_ge(d_lo, q + 1)
                for j in range(NT):
                    t, half = j // 2, j % 2
                    pe.wait_ge(d_add, NT * (q + 1) + max(j - DB + 1, 0))
                    for i in range(2):
                        for n, (l, r) in enumerate(((hid_hi, dh), (hid_hi, dl), (hid_lo, dh))):
                            last = nc.tensor.matmul(dp[:, j % DB, :], l[:, i, P * t:P * t + P],
                                                    r[:, i, NB * half:NB * half + NB],
                                                    start=(i == 0 and n == 0), stop=(i == 1 and n == 2))
                    last.then_inc(d_mm, 1)

            def modulate(r, i, first=False):
                if ada is None:
                    return
                pe.wait_ge(a_ld, 32 * r + 16 * i + 16)
                if not first:
                    pe.wait_ge(a_row, 2 * r + i)
                for n in range(KT // 4):
                    for j in range(4):
                        k = KT // 4 * j + n
                        last = nc.tensor.matmul(am[32 * j:32 * j + 1, i, :], cs[:, k:k + 1], aw[:, k, :],
                                                start=(n == 0), stop=(n == KT // 4 - 1),
                                                skip_group_check=True)
                last.then_inc(a_mm, 1)

            if begun is not None:
                pe.sem_inc(gu_mm, 1)
            gate_up(0, 0, True, lambda n: modulate(n // 2, n % 2, n == 0), (0, 1) if begun is None else (1,))
            gate_up(0, 1, False, lambda n: modulate(2 + n // 2, n % 2))
            with pe.Fori(1, PAIRS) as q:
                gate_up(q, 0, False)
                modulate(q + EARLY // 2, 0)
                down(q - 1)
                gate_up(q, 1, False)
                modulate(q + EARLY // 2, 1)
            down(PAIRS - 1)


def band_start(t):
    return min(max(P * t - HD, 0), S - BAND)


def value_tiles_a():
    return ([(P * n, 1) for n in NAT] + [(o, 1) for o in OFFS]
            + [(CL * P * c + r, CL) for r in range(CL) for c in range(2)])


def products(dil, half):
    out = []
    if not dil:
        for cb in range(CBS // HALVES):
            for rc in range(ROWS // RC):
                users = [(cb * RBS + rb, rc - rb) for rb in range(RBS) if 0 <= rc - rb < KR // RC]
                out.append((rc * CBS + half * CBS // HALVES + cb, users, None))
        return out
    for v, (start, step) in enumerate(value_tiles_a()):
        if step != 1:
            continue
        users = []
        for t in range(TT // HALVES):
            w0 = band_start(half * TT // HALVES + t)
            users += [(t, ch) for ch in range(BAND // P) if w0 + P * ch == start]
        if users:
            out.append((v, users, None))
    for r in range(CL):
        for c in range(CK // P):
            out.append((len(NAT) + len(OFFS) + 2 * r + c, [(t, BAND // P + c) for t in range(TT // HALVES)], r))
    return out


def load_projections(eng, raw, w_in, at, loaded):
    w_v = w_in.rearrange("(k p) n -> p k n", p=P)
    for j in range(3):
        eng.dma_start(raw[:, :, j, :], w_v[:, :, bass.ds(at + j * D // 2, P)]).then_inc(loaded, 16)


def attention_phase(nc, top, tag, w_in, w_at, w_next, y_at, ut_hi, ut_lo, scratch, ident, bias_in, tab, y_t,
                    weights, pj, begun, ahead=None):
    dil = tag == "a"
    NC = 4 if dil else 3
    W = NC * P
    HT = TT // HALVES
    NV = A_VT if dil else (ROWS // RC) * CBS
    VB = 4
    NVG = -(-NV // VB)
    UN = 2 * HT
    NU = HALVES * UN
    NPJ = 3 * HALVES
    LAG = 3
    PROJECTED = (2, 1, 0)

    def sem(name):
        return top.sem(f"{tag}_{name}")

    w_ld, b_ld, w_hi, w_lo = sem("w_ld"), sem("b_ld"), sem("w_hi"), sem("w_lo")
    zeroed, pj_mm, pj_v, pj_s = sem("zeroed"), sem("pj_mm"), sem("pj_v"), sem("pj_s")
    v_tr, v_out, qk, low, exped = sem("v_tr"), sem("v_out"), sem("qk"), sem("low"), sem("exped")
    rec, divided, p_tr, p_out = sem("rec"), sem("divided"), sem("p_tr"), sem("p_out")
    pv, y_out, y_st, b_ready, r_ld = sem("pv"), sem("y_out"), sem("y_st"), sem("b_ready"), sem("r_ld")
    with ExitStack() as st:
        a = Parts(nc, st)
        raw, wh, wl = weights
        q = a.sb(tag + "_q", [P, 2, S])
        kv = a.sb(tag + "_kv", [P, 2 if dil else 1, S])
        t_s = a.sb(tag + "_t", [P, 2, W])
        ex = a.sb(tag + "_ex", [P, 2, W])
        pn = a.sb(tag + "_pn", [P, 2, W])
        sm = a.sb(tag + "_sm", [P, 2, 4])
        y = a.sb(tag + "_y", [P, S])
        if dil:
            kc = a.sb("a_kc", [P, CL, CK])
            bias = a.sb("a_bias", [P, A_PAD])
        else:
            runs = a.sb("b_runs", [P, 2, RUN_R * TAB_W])
            mask = a.sb("b_mask", [P, RBS * 3, B_K])
            bias = a.sb("b_bias", [P, 2, RBS * 3, B_K])
            vc = a.sb("b_vc", [P, CBS, ROWS, KC])
        flat = scratch[:, :, :].rearrange("p t d -> p (t d)")
        pt_flat = flat[:, 0:2 * HT * W].rearrange("p (h x) -> p h x", h=2)
        pt = pt_flat.rearrange("p h (t c q) -> p h t c q", t=HT, c=NC)
        vt = flat[:, TT * D // 2:TT * D // 2 + NV * P].rearrange("p (v f) -> p v f", v=NV)
        sc = a.ps(tag + "_sc", [P, 2, NB])
        tr = a.ps(tag + "_tr", [P, 2, NB])
        o = a.ps(tag + "_o", [P, 2, NB])
        block = st.enter_context(nc.Block())

        def project(p, j, eng):
            on_vector = eng is nc.vector
            copy = nc.vector.tensor_copy if on_vector else nc.scalar.copy
            i = 0 if on_vector else 1
            for half in range(HALVES) if j == 0 else [i]:
                eng.wait_ge(pj_mm, NPJ * p + 2 * PROJECTED.index(j) + half + 1)
                if j == 0:
                    rows = slice(HD * i, HD * i + HD)
                    if dil:
                        to = q[rows, i, NB * half:NB * half + NB].rearrange("p (t r m) -> p t r m", r=CL, m=CQ)
                        of = pj[rows, half, :].rearrange("p (t m r) -> p t r m", r=CL, m=CQ)
                    else:
                        to = q[rows, i, :].rearrange("p (c b r w) -> p c b r w", c=CBS, b=RBS,
                                                     r=QR)[:, :, half]
                        of = pj[rows, half, :].rearrange("p (r c w) -> p c r w", r=QR, c=CBS)
                    if on_vector:
                        ins = nc.vector.tensor_scalar(to, of, -HD ** -0.5, None, ALU.mult)
                    else:
                        ins = nc.scalar.activation(to, of, ACT.Copy, scale=-HD ** -0.5)
                elif j == 2 and not dil:
                    for cb in range(CBS):
                        ins = copy(vc[:, cb, QR * half:QR * half + QR, :],
                                   pj[:, half, :].rearrange("p (r c) -> p r c", c=COLS)[:, :, KC0[cb]:KC0[cb] + KC])
                else:
                    if j == 1 and dil:
                        m0 = CK // HALVES * half
                        copy(kc[:, :, m0:m0 + CK // HALVES], pj[:, half, :].rearrange("p (m r) -> p r m", r=CL))
                    ins = copy(kv[:, j - 1, NB * half:NB * half + NB], pj[:, half, :])
                ins.then_inc(pj_v if on_vector else pj_s, 1)

        def over_pairs(engine, pair):
            pair(0, True, False)
            with engine.Fori(1, HP - 1) as p:
                pair(p, False, False)
            pair(HP - 1, False, True)

        @block.sync
        def _(sp):
            def pair(p, first, last):
                if not last or w_next is not None:
                    if not first:
                        sp.wait_ge(w_lo, p)
                    load_projections(sp, raw, w_in, w_next if last else (p + 1) * P + w_at, w_ld)
                if last and ahead is not None:
                    sp.wait_ge(w_lo, HP - 1)
                    ahead[0](sp)
                if dil:
                    if not first:
                        sp.wait_ge(low, NU * p)
                    sp.dma_start(bias[:, :], bias_in[:, bass.ds(p, 1), :].rearrange("p o w -> p (o w)")
                                 ).then_inc(b_ld, 16)
                sp.wait_ge(y_out, HALVES * (p + 1))
                sp.dma_start(y_t[bass.ds(p + y_at, 1)].rearrange("o p s -> (o p) s"), y[:, :]
                             ).then_inc(y_st, 16)

            if not dil:
                sp.dma_start(mask[:, :, :], bias_in).then_inc(b_ld, 16)
            over_pairs(sp, pair)
            sp.wait_ge(y_st, 16 * HP)

        @block.gpsimd
        def _(pool):
            for i in range(2):
                nc.gpsimd.memset(q[HD * (1 - i):HD * (2 - i), i, :], 0.0).then_inc(zeroed, 1)
            if dil:
                return
            pool.wait_ge(zeroed, 2)
            for p in range(HP):
                if p >= 1:
                    pool.wait_ge(b_ready, 2 * RBS * 3 * p)
                for rr in range(QR):
                    at = (QR - 1 - rr) * TAB_W
                    pool.dma_start(runs[QC * rr:QC * rr + QC, :, 0:RUN],
                                   tab[:, 2 * p:2 * p + 2, at:at + RUN]).then_inc(r_ld, 16)
                pool.wait_ge(r_ld, 16 * QR * (p + 1))
                if p == 0:
                    pool.wait_ge(b_ld, 16)
                else:
                    pool.wait_ge(low, NU * p)
                for i in range(2):
                    for rb in range(RBS):
                        for kind in range(3):
                            r0, c0 = 4 - 4 * rb, QC - 8 * kind
                            run = runs[:, i, :].rearrange("p (r w) -> p r w", w=TAB_W)[
                                :, r0:r0 + KR, c0:c0 + KC]
                            m = mask[:, rb * 3 + kind].rearrange("p (r w) -> p r w", w=KC)
                            b = bias[:, i, rb * 3 + kind].rearrange("p (r w) -> p r w", w=KC)
                            nc.gpsimd.tensor_tensor(b, run, m, ALU.add).then_inc(b_ready, 1)
            if ahead is not None:
                ahead[1](pool)

        @block.scalar
        def _(act):
            def split(p):
                act.wait_ge(w_ld, 48 * p)
                act.wait_ge(pj_mm, NPJ * p)
                nc.scalar.copy(wh[:, :, :, :], raw[:, :, :, :]).then_inc(w_hi, 1)

            def exponential(p, m, first):
                u, b = NU * p + m, m % 2
                act.wait_ge(low, u + 1)
                if not (first and m < 2):
                    act.wait_ge(divided, u - 1)
                nc.scalar.activation(ex[:, b, :], t_s[:, b, :], ACT.Exp, bias=sm[:, b, 0:1], scale=-1.0,
                                     accum_out=sm[:, b, 1:2]).then_inc(exped, 1)

            def turned_out(p, m, first):
                act.wait_ge(p_tr, NU * p + m + 1)
                half, n = m // UN, m % UN
                if n == 0 and not (first and half == 0):
                    act.wait_ge(pv, HALVES * p + half)
                nc.scalar.copy(pt[:, n % 2, n // 2], tr[:, n % 2, 0:W].rearrange("p (c q) -> p c q", c=NC)
                               ).then_inc(p_out, 1)

            def pair(p, first, last):
                project(p, 1, act)
                project(p, 0, act)
                for m in range(NU + LAG):
                    if m < NU:
                        exponential(p, m, first)
                    if m == UN + LAG and not (last and w_next is None):
                        split(p + 1)
                    if m >= LAG:
                        turned_out(p, m - LAG, first)
                if not last:
                    project(p + 1, 2, act)

            project(0, 2, act)
            over_pairs(act, pair)

        @block.vector
        def _(dve):
            def split(p):
                dve.wait_ge(w_hi, p)
                nc.vector.tensor_tensor(wl[:, :, :, :], raw[:, :, :, :], wh[:, :, :, :].bitcast(F32),
                                        ALU.subtract).then_inc(w_lo, 1)

            def values(p):
                for g in range(NVG):
                    n = min(VB, NV - VB * g)
                    dve.wait_ge(v_tr, NVG * p + g + 1)
                    nc.vector.tensor_copy(vt[:, VB * g:VB * g + n, :],
                                          tr[:, g % 2, 0:P * n].rearrange("p (v f) -> p v f", v=n)
                                          ).then_inc(v_out, 1)

            def tile_bias(m):
                t, i = m // 2, m % 2
                if dil:
                    band = band_start(t) - P * t + P
                    at = A_W * i + band
                    step = BAND_W + (CK - CQ) - CQ * t - band
                    return bias[:, at:at + 2 * step].rearrange("p (a s) -> p a s", s=step)[:, :, 0:BAND]
                cb, rb = t // RBS, t % RBS
                return bias[:, i, rb * 3 + KIND[cb]]

            def step(p, m, first):
                u, b = NU * p + m, m % 2
                if m < NU:
                    dve.wait_ge(qk, u + 1)
                if m == 0 and dil:
                    dve.wait_ge(b_ld, 16 * (p + 1))
                if m == 0 and not dil:
                    dve.wait_ge(b_ready, 2 * RBS * 3 * (p + 1))
                if not (first and m < 2):
                    dve.wait_ge(exped, u - 1)
                if m < 2:
                    nc.vector.memset(sm[:, b, 3:4], 0.0)
                else:
                    nc.vector.reciprocal(sm[:, b, 2:3], sm[:, b, 1:2]).then_inc(rec, 1)
                if m < NU:
                    of, to = sc[:, b, 0:W], t_s[:, b, :]
                    if dil:
                        of, to = (x.rearrange("p (a k) -> p a k", a=2) for x in (of, to))
                    nc.vector.tensor_tensor_reduce(to, of, tile_bias(m), 1.0, 3e38, ALU.add, ALU.min,
                                                   sm[:, b, 0:1]).then_inc(low, 1)
                if m < 2:
                    return
                dve.wait_ge(rec, u - 1)
                if not (first and m < 4):
                    dve.wait_ge(p_tr, u - 3)
                nc.vector.tensor_scalar(pn[:, b, :], ex[:, b, :], sm[:, b, 2:3], None,
                                        ALU.mult).then_inc(divided, 1)

            def output(p, half, first):
                dve.wait_ge(pv, HALVES * p + half + 1)
                if half == 0 and not first:
                    dve.wait_ge(y_st, 16 * p)
                if dil:
                    to = y[:, NB * half:NB * half + NB].rearrange("p (t m r) -> p t r m", r=CL, m=CQ)
                    of = o[:, half, :].rearrange("p (t r m) -> p t r m", r=CL, m=CQ)
                    ins = nc.vector.tensor_copy(to, of)
                else:
                    n = CBS // HALVES
                    to = y[:, :].rearrange("p (b r c w) -> p b r c w", b=RBS, r=QR, c=CBS)
                    of = o[:, half, :].rearrange("p (c b r w) -> p c b r w", c=n, b=RBS, r=QR)
                    for c in range(n):
                        for b in range(RBS):
                            ins = nc.vector.tensor_copy(to[:, b, :, n * half + c], of[:, c, b])
                ins.then_inc(y_out, 1)

            def pair(p, first, last):
                project(p, 1, dve)
                values(p)
                project(p, 0, dve)
                for m in range(NU + 2):
                    step(p, m, first)
                    if m == UN + LAG and not (last and w_next is None):
                        split(p + 1)
                    if m == UN + LAG + 2:
                        output(p, 0, first)
                if not last:
                    project(p + 1, 2, dve)
                output(p, 1, first)

            project(0, 2, dve)
            over_pairs(dve, pair)

        @block.tensor
        def _(pe):
            def out_of_banks(p, n):
                by_vector, by_scalar = (0, 1, 1, 2, 2, 3, 4)[n], (0, 0, 1, 1, 2, 3, 4)[n]
                pe.wait_ge(pj_v, 4 * p + by_vector)
                if not (isinstance(p, int) and p == 0 and by_scalar == 0):
                    pe.wait_ge(pj_s, 4 * p + by_scalar)

            def project(p, j, half, first=False):
                x = 2 * PROJECTED.index(j) + half
                if x == 0 and not first:
                    pe.wait_ge(w_lo, p)
                if not (first and x < 2):
                    if x == 0:
                        out_of_banks(p - 1, NPJ - 1)
                    elif x > 1:
                        out_of_banks(p, x - 1)
                    else:
                        out_of_banks(p - 1, NPJ)
                for k in range(KT):
                    for n, (l, r) in enumerate(((wh, ut_hi), (wh, ut_lo), (wl, ut_hi))):
                        last = nc.tensor.matmul(pj[:, half, :], l[:, k, j, :],
                                                r[:, k, NB * half:NB * half + NB],
                                                start=(k == 0 and n == 0), stop=(k == KT - 1 and n == 2))
                last.then_inc(pj_mm, 1)

            def value_source(v):
                if dil:
                    start, step = value_tiles_a()[v]
                    return kv[:, 1, start:start + step * (P - 1) + 1:step]
                rc, cb = v // CBS, v % CBS
                return vc[:, cb, RC * rc:RC * rc + RC, :].rearrange("p r c -> p (r c)")

            def values(p, first):
                out_of_banks(p, 2)
                if not first:
                    pe.wait_ge(p_out, NU * p)
                for g in range(NVG):
                    if g >= 2:
                        pe.wait_ge(v_out, NVG * p + g - 1)
                    for v in range(VB * g, min(VB * g + VB, NV)):
                        at = P * (v - VB * g)
                        last = nc.tensor.transpose(tr[:, g % 2, at:at + P], value_source(v), ident[:, :])
                    last.then_inc(v_tr, 1)

            def score(p, m, first):
                u, b = NU * p + m, m % 2
                t, i = m // 2, m % 2
                if not (first and m < 2):
                    pe.wait_ge(low, u - 1)
                if dil:
                    w0 = band_start(t)
                    nc.tensor.matmul(sc[:, b, 0:BAND], q[:, i, P * t:P * t + P], kv[:, 0, w0:w0 + BAND],
                                     start=True, stop=True, skip_group_check=True)
                    for r in range(CL):
                        last = nc.tensor.matmul(sc[CQ * r:CQ * r + CQ, b, BAND:BAND + CK],
                                                q[:, i, P * t + CQ * r:P * t + CQ * r + CQ], kc[:, r, :],
                                                start=True, stop=True, skip_group_check=True)
                else:
                    cb, rb = t // RBS, t % RBS
                    grid = kv[:, 0, :].rearrange("p (r c) -> p r c", c=COLS)
                    last = nc.tensor.matmul(sc[:, b, 0:W], q[:, i, P * t:P * t + P],
                                            grid[:, 4 * rb:4 * rb + KR, KC0[cb]:KC0[cb] + KC],
                                            start=True, stop=True)
                last.then_inc(qk, 1)

            def turn(p, m, first):
                u, b = NU * p + m, m % 2
                pe.wait_ge(divided, u + 1)
                if m < 2:
                    pe.wait_ge(v_out, NVG * (p + 1))
                else:
                    pe.wait_ge(p_out, u - 1)
                for c in range(NC):
                    last = nc.tensor.transpose(tr[:, b, P * c:P * c + P], pn[:, b, P * c:P * c + P],
                                               ident[:, :])
                last.then_inc(p_tr, 1)

            def multiply(p, half, first):
                pe.wait_ge(p_out, NU * p + UN * (half + 1))
                if not first:
                    pe.wait_ge(y_out, HALVES * (p - 1) + half + 1)
                todo = products(dil, half)
                for n, (v, users, cls) in enumerate(todo):
                    for i in range(2):
                        to = o[HD * i:HD * i + HD, half, :]
                        if cls is not None:
                            to = to.rearrange("p (t r m) -> p t r m", r=CL, m=CQ)[:, :, cls]
                            of = pt[:, i, :, users[0][1], CQ * cls:CQ * cls + CQ]
                        else:
                            t, ch = users[0]
                            to = to[:, P * t:P * (t + len(users))]
                            of = pt[:, i, t, ch]
                            if len(users) == 2:
                                at, step = (t * NC + ch) * P, (NC - 1) * P
                                of = pt_flat[:, i, at:at + 2 * step].rearrange(
                                    "p (a s) -> p a s", s=step)[:, :, 0:P]
                        last = nc.tensor.matmul(to, vt[:, v, HD * i:HD * i + HD], of, start=(n == 0),
                                                stop=(n == len(todo) - 1), skip_group_check=True)
                last.then_inc(pv, 1)

            def pair(p, first, last):
                for half in range(HALVES):
                    project(p, 1, half)
                values(p, first)
                for half in range(HALVES):
                    project(p, 0, half)
                out_of_banks(p, NPJ)
                for m in range(NU + LAG):
                    if m < NU:
                        score(p, m, first)
                    if m >= LAG:
                        turn(p, m - LAG, first)
                    if NU - 1 <= m < NU - 1 + HALVES and not last:
                        project(p + 1, 2, m - (NU - 1))
                    if m - LAG == UN:
                        multiply(p, 0, first)
                multiply(p, 1, first)

            if begun:
                pe.sem_inc(pj_mm, 1)
            for half in [1] if begun else range(HALVES):
                project(0, 2, half, True)
            pe.wait_ge(zeroed, 2)
            over_pairs(pe, pair)


def output_projection_ahead(nc, w_out, gate, w, gates, loaded, scaled):
    def load(sp):
        for b in range(2):
            sp.dma_start(w[:, b, :], w_out[P * b:P * b + P, :]).then_inc(loaded, 16)
        sp.dma_start(gates, gate.broadcast_to([P, D])).then_inc(loaded, 16)

    def scale(pool):
        pool.wait_ge(loaded, 48)
        for b in range(2):
            nc.gpsimd.tensor_tensor(w[:, b, :], w[:, b, :], gates, ALU.mult).then_inc(scaled, 1)

    return load, scale


def output_projection_phase(nc, top, w_out, y_t, h_t, ut_hi, ut_lo, acc, w, gates, lng, lnb):
    y_ld = [top.sem(f"o_y_ld{b}") for b in range(2)]
    w_ld = [top.sem(f"o_w_ld{b}") for b in range(2)]
    h_ld, scaled = top.sem("o_h_ld"), top.sem("o_scaled")
    y_hi, y_lo, w_hi, w_lo = top.sem("o_y_hi"), top.sem("o_y_lo"), top.sem("o_w_hi"), top.sem("o_w_lo")
    mm, out = top.sem("o_mm"), top.sem("o_out")
    NT = TT * HALVES
    BANKS = 8
    with ExitStack() as st:
        a = Parts(nc, st)
        y = a.sb("o_y", [P, 2, S])
        wh = a.sb("o_wh", [P, KT, D], F32R)
        wl = a.sb("o_wl", [P, KT, D], F32R)
        ps = a.ps("o_ps", [P, BANKS, NB])
        leaving = Leaving(nc, top, a, "o", acc, a.sb("o_rows", [P, 2, D]), lng, lnb)
        block = st.enter_context(nc.Block())

        @block.sync
        def _(sp):
            for k in range(KT):
                b = k % 2
                if k >= 2:
                    sp.wait_ge(y_lo, k - 1)
                    sp.wait_ge(w_lo, k - 1)
                    sp.dma_start(w[:, b, :], w_out[P * k:P * k + P, :]).then_inc(w_ld[b], 16)
                sp.dma_start(y[:, b, :], y_t[k]).then_inc(y_ld[b], 16)
            sp.dma_start(acc[:, :, :], h_t.rearrange("(t p) d -> p t d", p=P)).then_inc(h_ld, 16)
            leaving.load(sp)

        @block.gpsimd
        def _(pool):
            for k in range(2, KT):
                pool.wait_ge(w_ld[k % 2], 16 * (k // 2))
                nc.gpsimd.tensor_tensor(w[:, k % 2, :], w[:, k % 2, :], gates, ALU.mult).then_inc(scaled, 1)
            leaving.affine(pool)

        @block.scalar
        def _(act):
            for k in range(KT):
                if k >= 2:
                    act.wait_ge(scaled, k - 1)
                nc.scalar.copy(wh[:, k, :], w[:, k % 2, :]).then_inc(w_hi, 1)
                act.wait_ge(y_ld[k % 2], 16 * (k // 2 + 1))
                nc.scalar.copy(ut_hi[:, k, :], y[:, k % 2, :]).then_inc(y_hi, 1)
            leaving.normalise(act)

        @block.vector
        def _(dve):
            for k in range(KT):
                dve.wait_ge(w_hi, k + 1)
                nc.vector.tensor_tensor(wl[:, k, :], w[:, k % 2, :], wh[:, k, :].bitcast(F32),
                                        ALU.subtract).then_inc(w_lo, 1)
                dve.wait_ge(y_hi, k + 1)
                nc.vector.tensor_tensor(ut_lo[:, k, :], y[:, k % 2, :], ut_hi[:, k, :].bitcast(F32),
                                        ALU.subtract).then_inc(y_lo, 1)
            dve.wait_ge(h_ld, 16)
            for j in range(NT):
                cols = slice(NB * (j % 2), NB * (j % 2) + NB)
                dve.wait_ge(mm, j + 1)
                nc.vector.tensor_tensor(acc[:, j // 2, cols], ps[:, j % BANKS, :], acc[:, j // 2, cols],
                                        ALU.add).then_inc(out, 1)
                if j % 2 == 1 and j >= BANKS:
                    for t in ([j // 2] if j > BANKS + 1 else range(BANKS // 2 + 1)):
                        dve.wait_ge(out, 2 * t + 2)
                        leaving.summed(dve, t)
                if j == NT - 3:
                    leaving.shifts(dve, range(leaving.ON_POOL, TT - 2))
            leaving.finish(dve, TT - 2)

        @block.tensor
        def _(pe):
            def block_of(j, k):
                t, half = j // 2, j % 2
                for n, (l, r) in enumerate(((ut_hi, wh), (ut_hi, wl), (ut_lo, wh))):
                    last = nc.tensor.matmul(ps[:, j % BANKS, :], l[:, k, P * t:P * t + P],
                                            r[:, k, NB * half:NB * half + NB],
                                            start=(k == 0 and n == 0), stop=(k == KT - 1 and n == 2))
                if k == KT - 1:
                    last.then_inc(mm, 1)

            for k in range(KT):
                pe.wait_ge(w_lo, k + 1)
                pe.wait_ge(y_lo, k + 1)
                for j in range(BANKS):
                    block_of(j, k)
            for j in range(BANKS, NT):
                pe.wait_ge(out, j - BANKS + 1)
                for k in range(KT):
                    block_of(j, k)


def kernel_program(nc, x, c, w_ada, b_ada, g1, u1, d1, w_in, rpb, w_out, g2, u2, d2, ln_g, ln_b,
                   ident_in, a_bias, b_mask, out):
    mods = nc.dram_tensor("mods", [1, N_MOD * D], F32, kind="Internal").ap()
    h_t = nc.dram_tensor("scaled_h_before_mix", [S, D], F32, kind="Internal").ap()
    y_t = nc.dram_tensor("mixed_turned", [KT, P, S], F32, kind="Internal").ap()
    tab = nc.dram_tensor("bias_table", [QC, HEADS, TAB_R * TAB_W], F32, kind="Internal").ap()
    ada_v = w_ada.rearrange("l (k p) n -> p (l k) n", p=P)
    with ExitStack() as st:
        top = Parts(nc, st)
        mod_col = top.sb("mod_col", [P, 3 * 2 * KT])
        ident = top.sb("ident", [P, P])
        cs = top.sb("silu_c", [P, KT])
        acc = top.sb("acc", [P, TT, D])
        ut_hi = top.sb("ut_hi", [P, KT, S], F32R)
        ut_lo = top.sb("ut_lo", [P, KT, S], F32R)
        common = (acc, mod_col, ident, ut_hi, ut_lo)

        def gate(j):
            return mods[:, (3 * j + 2) * D:(3 * j + 3) * D]

        def first_products(k, wh, wl, gu):
            for g in range(2):
                for n, (l, r) in enumerate(((wh, ut_hi), (wh, ut_lo), (wl, ut_hi))):
                    nc.tensor.matmul(gu[:, 0, g, :], l[:, 0, k, g, :], r[:, k, 0:NB], start=(k == 0 and n == 0),
                                     stop=(k == KT - 1 and n == 2))

        def first_values(k, wh, wl, pj):
            for n, (l, r) in enumerate(((wh, ut_hi), (wh, ut_lo), (wl, ut_hi))):
                nc.tensor.matmul(pj[:, 0, :], l[:, k, 2, :], r[:, k, 0:NB], start=(k == 0 and n == 0),
                                 stop=(k == KT - 1 and n == 2))

        def ffn(tag, weights, j, ada, start, out):
            views = ffn_views(*weights)
            with ExitStack() as inner:
                own = Parts(nc, inner)
                first = top.sem(tag + "_first")
                gu = own.ps(tag + "_gu", [P, 2, 2, NB])
                raw = own.sb(tag + "_raw", [P, KT, 2, 2 * P])
                raw_d = own.sb(tag + "_raw_d", [P, 2, D])
                with ExitStack() as beginning:
                    nrm = None
                    if start is not None:
                        nrm = Parts(nc, beginning).sb(tag + "_nrm", [P, TT, D])
                        with nc.cleanup_on_exit():
                            start(nrm)
                    ahead, begun = {}, None
                    if start is None:
                        begun = wh, wl = ffn_weights(own, tag)
                        ahead = dict(split_first=(raw[:, :, :, 0:P], wh[:, 0], wl[:, 0]),
                                     begin=lambda k: first_products(k, wh, wl, gu))
                    with nc.cleanup_on_exit():
                        boundary_phase(nc, top, tag + "b", *common, enter=j, nrm=nrm,
                                       prefetch=ffn_prefetch(views, raw, raw_d, first), loaded=[(first, 48)],
                                       **ahead)
                with nc.cleanup_on_exit():
                    ffn_phase(nc, top, tag, views, raw, raw_d, gate(j), 0.5, ut_hi, ut_lo, acc, ada,
                              lng=ln_g[0, j:j + 1, :], lnb=ln_b[0, j:j + 1, :], out=out, gu=gu,
                              begun=begun)

        ffn("f1", (g1, u1, d1), 0, (cs, ada_v, b_ada, mods),
            lambda nrm: modulation_phase(nc, top, c, ada_v, b_ada, ident_in, rpb, mods, ident, cs, tab, mod_col, x,
                                         acc, nrm), None)
        with ExitStack() as inner:
            own = Parts(nc, inner)
            raw = own.sb("in_raw", [P, KT, 3, P])
            flat = raw[:, :, :, :].rearrange("p k j n -> p (k j n)")
            w_o, gates_o = flat[:, 0:2 * D].rearrange("p (b n) -> p b n", b=2), flat[:, 2 * D:3 * D]
            with ExitStack() as parts:
                own = Parts(nc, parts)
                wh = own.sb("in_wh", [P, KT, 3, P], F32R)
                wl = own.sb("in_wl", [P, KT, 3, P], F32R)
                weights = tuple(x_[:, :, :, :] for x_ in (raw, wh, wl))
                pj = own.ps("in_pj", [P, 2, NB])
                first = top.sem("in_first")
                at_b = 3 * D // 2
                with nc.cleanup_on_exit():
                    boundary_phase(nc, top, "b1", *common, enter=1, store=h_t, mods=mods,
                                   prefetch=lambda sp: load_projections(sp, raw, w_in, 0, first),
                                   loaded=[(first, 48)], split_first=weights,
                                   begin=lambda k: first_values(k, wh, wl, pj))
                with nc.cleanup_on_exit():
                    attention_phase(nc, top, "a", w_in, 0, at_b, 0, ut_hi, ut_lo, acc, ident, a_bias, None, y_t, weights,
                                    pj, True)
                with nc.cleanup_on_exit():
                    attention_phase(nc, top, "b", w_in, at_b, None, HP, ut_hi, ut_lo, acc, ident, b_mask, tab, y_t,
                                    weights, pj, False,
                                    output_projection_ahead(nc, w_out, gate(1), w_o, gates_o,
                                                            top.sem("o_first"), top.sem("o_first_scaled")))
            with nc.cleanup_on_exit():
                output_projection_phase(nc, top, w_out, y_t, h_t, ut_hi, ut_lo, acc, w_o, gates_o,
                                        lng=ln_g[0, 1:2, :], lnb=ln_b[0, 1:2, :])
        ffn("f2", (g2, u2, d2), 2, None, None, out)


def kernel(x, c, w_ada, b_ada, ffn1_w_gate, ffn1_w_up, ffn1_w_down, w_in, rpb, w_out,
           ffn2_w_gate, ffn2_w_up, ffn2_w_down, ln_g, ln_b):
    import concourse.bacc as bacc
    from concourse.bass_utils import run_bass_kernel_spmd

    nc = bacc.Bacc("TRN2", target_bir_lowering=False, num_devices=1)
    arrays = dict(x=x, c=c, w_ada=w_ada, b_ada=b_ada, ffn1_w_gate=ffn1_w_gate, ffn1_w_up=ffn1_w_up,
                  ffn1_w_down=ffn1_w_down, w_in=w_in, rpb=rpb, w_out=w_out, ffn2_w_gate=ffn2_w_gate,
                  ffn2_w_up=ffn2_w_up, ffn2_w_down=ffn2_w_down, ln_g=ln_g, ln_b=ln_b)
    arrays.update(identity=np.eye(P, dtype=np.float32), dilated_bias=dilated_bias(),
                  window_masks=window_masks())
    arrays = {n: np.ascontiguousarray(v) for n, v in arrays.items()}
    d = {n: nc.dram_tensor("in_" + n, list(v.shape), F32, kind="ExternalInput").ap()
         for n, v in arrays.items()}
    out = nc.dram_tensor("out", [1, S, D], F32, kind="ExternalOutput").ap()
    kernel_program(nc, d["x"][0], d["c"], d["w_ada"], d["b_ada"], d["ffn1_w_gate"][0], d["ffn1_w_up"][0],
                   d["ffn1_w_down"][0], d["w_in"][0], d["rpb"], d["w_out"][0], d["ffn2_w_gate"][0],
                   d["ffn2_w_up"][0], d["ffn2_w_down"][0], d["ln_g"], d["ln_b"], d["identity"],
                   d["dilated_bias"], d["window_masks"], out[0])
    got = run_bass_kernel_spmd(nc, [{"in_" + n: v for n, v in arrays.items()}], core_ids=[0])
    return got.results[0]["out"]
```
